# Optimizing a Trainium2 kernel written in Bass

```python
import jax
import jax.numpy as jnp
from jax import lax
import numpy as np
import math
import jax, jax.numpy as jnp

D_MODEL = 1024
BATCH = 1
SEQ = 256
DEPTH = 2

GRID_W = 64
CTX_LEN = 256
NORM_EPS = 1e-6
ROPE_THETA = 10000.0
Q_BLOCK = 128

GDN_HEADS = 8
GDN_DK = 64
GDN_DV = 64
GDN_CONV = 5
GDN_CHUNK = 64
GDN_QK_W = GDN_HEADS * GDN_DK
GDN_V_W = GDN_HEADS * GDN_DV

MLA_HEADS = 8
MLA_NOPE = 64
MLA_ROPE = 32
MLA_V = 64
MLA_Q_LORA = 256
MLA_KV_LORA = 128

NA_HEADS = 8
NA_DIM = 64
NA_WIN_H = 8
NA_WIN_W = 16
NA_W = NA_HEADS * NA_DIM

GQA_HEADS = 8
GQA_KV_HEADS = 2
GQA_DIM = 64

D_FF = -(-(8 * D_MODEL) // (3 * 256)) * 256

EVEN_SPLITS = (2 * GDN_QK_W + GDN_V_W, GDN_V_W, 2 * GDN_HEADS, 2 * GDN_HEADS, MLA_Q_LORA, MLA_KV_LORA, MLA_ROPE)
ODD_SPLITS = (NA_W, NA_W, NA_W, GQA_HEADS * GQA_DIM, GQA_KV_HEADS * GQA_DIM, GQA_KV_HEADS * GQA_DIM)
IN_EVEN = sum(EVEN_SPLITS)
IN_ODD = sum(ODD_SPLITS)
MIX_EVEN = GDN_V_W + MLA_HEADS * MLA_V
MIX_ODD = NA_W + GQA_HEADS * GQA_DIM
N_EVEN = (DEPTH + 1) // 2
N_ODD = DEPTH // 2


def split_cols(z, sizes):
    offs = [int(o) for o in np.cumsum(sizes)[:-1]]
    return jnp.split(z, offs, axis=-1)

def to_heads(t, n):
    return t.reshape(t.shape[0], t.shape[1], n, -1)

def rms_norm(x, g):
    xf = x.astype(jnp.float32)
    y = xf * lax.rsqrt(jnp.mean(xf * xf, -1, keepdims=True) + NORM_EPS)
    return (y * g.astype(jnp.float32)).astype(x.dtype)

def l2_normalize(x):
    xf = x.astype(jnp.float32)
    return (xf * lax.rsqrt(jnp.sum(xf * xf, -1, keepdims=True) + NORM_EPS)).astype(x.dtype)

def modulate(h, shift, scale):
    return h * (1.0 + scale) + shift

def swiglu(u, w_gate, w_up, w_down):
    return (jax.nn.silu(u @ w_gate) * (u @ w_up)) @ w_down

def axial_rope(n_tokens, rot_dim):
    t = jnp.arange(n_tokens, dtype=jnp.int32)
    row = (t // GRID_W).astype(jnp.float32)
    col = (t % GRID_W).astype(jnp.float32)
    n_freq = rot_dim // 4
    inv_freq = ROPE_THETA ** (-jnp.arange(n_freq, dtype=jnp.float32) / n_freq)
    ang = jnp.concatenate([row[:, None] * inv_freq, col[:, None] * inv_freq], -1)
    return jnp.cos(ang), jnp.sin(ang)

def apply_rope(x, cos, sin):
    half = x.shape[-1] // 2
    x1, x2 = x[..., :half], x[..., half:]
    cs, sn = cos[None, :, None, :], sin[None, :, None, :]
    return jnp.concatenate([x1 * cs - x2 * sn, x2 * cs + x1 * sn], -1).astype(x.dtype)

def short_conv(x, w):
    n_tap = w.shape[0]
    pad = n_tap // 2
    t_len = x.shape[1]
    xp = jnp.pad(x, ((0, 0), (pad, pad), (0, 0)))
    out = xp[:, 0:t_len] * w[0]
    for j in range(1, n_tap):
        out = out + xp[:, j:j + t_len] * w[j]
    return out

def blocked_attention(q, k, v, scale):
    b, tq, h, d = q.shape
    hk = k.shape[2]
    grp = h // hk
    nb = tq // Q_BLOCK
    qb = q.reshape(b, nb, Q_BLOCK, hk, grp, d).transpose(1, 0, 2, 3, 4, 5)

    def one_block(q_i):
        s = jnp.einsum('bqkgd,bskd->bkgqs', q_i, k).astype(jnp.float32) * scale
        p = jax.nn.softmax(s, axis=-1).astype(v.dtype)
        return jnp.einsum('bkgqs,bskd->bqkgd', p, v)

    o = lax.map(one_block, qb)
    return o.transpose(1, 0, 2, 3, 4, 5).reshape(b, tq, h, v.shape[-1])

def delta_rule_chunked(q, k, v, g, beta, s0):
    f32 = jnp.float32
    b, t_len, h, dk = q.shape
    dv = v.shape[-1]
    n = t_len // GDN_CHUNK
    cl = GDN_CHUNK

    def chunks(t):
        return jnp.moveaxis(t.astype(f32).reshape(b, n, cl, h, *t.shape[3:]), 3, 1)

    qc, kc, vc, gch, bc = chunks(q), chunks(k), chunks(v), chunks(g), chunks(beta)
    gc = jnp.cumsum(gch, -1)
    tril = jnp.tril(jnp.ones((cl, cl), bool))
    strict = jnp.tril(jnp.ones((cl, cl), bool), -1)
    decay = jnp.exp(jnp.where(tril, gc[..., :, None] - gc[..., None, :], -jnp.inf))
    kb = kc * bc[..., None]
    vb = vc * bc[..., None]
    m = jnp.where(strict, jnp.einsum('bhncd,bhnsd->bhncs', kb, kc) * decay, 0.0)
    eye = jnp.eye(cl, dtype=f32)
    tmat = lax.linalg.triangular_solve(m + eye, jnp.broadcast_to(eye, m.shape), left_side=True,
                                       lower=True, unit_diagonal=True)
    u = jnp.einsum('bhncs,bhnsv->bhncv', tmat, vb)
    w = jnp.einsum('bhncs,bhnsk->bhnck', tmat, kb * jnp.exp(gc)[..., None])
    qk = jnp.einsum('bhncd,bhnsd->bhncs', qc, kc) * decay
    q_dec = qc * jnp.exp(gc)[..., None]
    k_dec = kc * jnp.exp(gc[..., -1:] - gc)[..., None]
    g_last = jnp.exp(gc[..., -1])
    xs = tuple(jnp.moveaxis(t, 2, 0) for t in (u, w, qk, q_dec, k_dec, g_last))

    def step(s, inp):
        u_i, w_i, qk_i, qd_i, kd_i, gl_i = inp
        v_new = u_i - jnp.einsum('bhck,bhkv->bhcv', w_i, s)
        o_i = jnp.einsum('bhck,bhkv->bhcv', qd_i, s) + jnp.einsum('bhcs,bhsv->bhcv', qk_i, v_new)
        s = s * gl_i[..., None, None] + jnp.einsum('bhck,bhcv->bhkv', kd_i, v_new)
        return s, o_i

    s_fin, o = lax.scan(step, s0.astype(f32), xs)
    return s_fin, o.transpose(1, 0, 3, 2, 4).reshape(b, t_len, h, dv)

def gdn_prepare(qkv, a, bt, conv_w, a_log, dt_bias):
    b, t_len, _ = qkv.shape
    qkv = jax.nn.silu(short_conv(qkv, conv_w))
    q, k, v = jnp.split(qkv, [GDN_QK_W, 2 * GDN_QK_W], axis=-1)
    q = l2_normalize(q.reshape(b, t_len, GDN_HEADS, GDN_DK)) * (GDN_DK ** -0.5)
    k = l2_normalize(k.reshape(b, t_len, GDN_HEADS, GDN_DK))
    v = v.reshape(b, t_len, GDN_HEADS, GDN_DV)
    a = a.reshape(b, t_len, 2, GDN_HEADS).astype(jnp.float32)
    bt = bt.reshape(b, t_len, 2, GDN_HEADS).astype(jnp.float32)
    g = -jnp.exp(a_log.astype(jnp.float32)) * jax.nn.softplus(a + dt_bias.astype(jnp.float32))
    return q, k, v, g, jax.nn.sigmoid(bt)

def gdn_bidirectional(lat, ctx):
    q_l, k_l, v_l, g_l, b_l = lat
    q_c, k_c, v_c, g_c, b_c = ctx
    s0 = jnp.zeros((q_l.shape[0], GDN_HEADS, GDN_DK, GDN_DV), jnp.float32)
    s_cf, oc_f = delta_rule_chunked(q_c, k_c, v_c, g_c[:, :, 0], b_c[:, :, 0], s0)
    _, ol_f = delta_rule_chunked(q_l, k_l, v_l, g_l[:, :, 0], b_l[:, :, 0], s_cf)
    fl = lambda t: jnp.flip(t, 1)
    s_cb, oc_b = delta_rule_chunked(fl(q_c), fl(k_c), fl(v_c), fl(g_c[:, :, 1]), fl(b_c[:, :, 1]), s0)
    _, ol_b = delta_rule_chunked(fl(q_l), fl(k_l), fl(v_l), fl(g_l[:, :, 1]), fl(b_l[:, :, 1]), s_cb)
    return ol_f + fl(ol_b), oc_f + fl(oc_b)

def gdn_output(o, gate, out_norm):
    b, t_len, h, dv = o.shape
    o = rms_norm(o.astype(gate.dtype), out_norm)
    return (o * jax.nn.silu(gate.reshape(b, t_len, h, dv))).reshape(b, t_len, h * dv)

def mla_q(q_down, q_norm, w_q_up, rope):
    b, t_len, _ = q_down.shape
    q = (rms_norm(q_down, q_norm) @ w_q_up).reshape(b, t_len, MLA_HEADS, MLA_NOPE + MLA_ROPE)
    if rope is None:
        return q
    return jnp.concatenate([q[..., :MLA_NOPE], apply_rope(q[..., MLA_NOPE:], *rope)], -1)

def mla_kv(kv_down, k_pe, kv_norm, w_kv_up, rope):
    b, t_len, _ = kv_down.shape
    kv = (rms_norm(kv_down, kv_norm) @ w_kv_up).reshape(b, t_len, MLA_HEADS, MLA_NOPE + MLA_V)
    k_pe = k_pe[:, :, None, :]
    if rope is not None:
        k_pe = apply_rope(k_pe, *rope)
    k = jnp.concatenate([kv[..., :MLA_NOPE], jnp.broadcast_to(k_pe, (b, t_len, MLA_HEADS, MLA_ROPE))], -1)
    return k, kv[..., MLA_NOPE:]

def neighbourhood_attention(q, k, v, k_ctx, v_ctx, rpb):
    b, s_len, h, d = q.shape
    rows = s_len // GRID_W
    kh = min(NA_WIN_H, rows)
    kw = NA_WIN_W
    nk = kh * kw
    r = jnp.arange(rows)
    col = jnp.arange(GRID_W)
    rs = jnp.clip(r - kh // 2, 0, rows - kh)
    cs = jnp.clip(col - kw // 2, 0, GRID_W - kw)
    kr = rs[:, None] + jnp.arange(kh)
    kc = cs[:, None] + jnp.arange(kw)
    idx = (kr[:, None, :, None] * GRID_W + kc[None, :, None, :]).reshape(rows, GRID_W * nk)
    dr = kr - r[:, None] + (NA_WIN_H - 1)
    dc = kc - col[:, None] + (NA_WIN_W - 1)
    bias = rpb[:, dr[:, None, :, None], dc[None, :, None, :]]
    bias = bias.reshape(h, rows, GRID_W, nk).transpose(1, 0, 2, 3).astype(jnp.float32)
    qr = q.reshape(b, rows, GRID_W, h, d).transpose(1, 0, 2, 3, 4)
    scale = d ** -0.5

    def row_block(inp):
        q_i, idx_i, b_i = inp
        kg = jnp.take(k, idx_i, axis=1).reshape(b, GRID_W, nk, h, d)
        vg = jnp.take(v, idx_i, axis=1).reshape(b, GRID_W, nk, h, d)
        s_loc = jnp.einsum('bqhd,bqnhd->bhqn', q_i, kg).astype(jnp.float32) * scale + b_i[None]
        s_ctx = jnp.einsum('bqhd,bshd->bhqs', q_i, k_ctx).astype(jnp.float32) * scale
        p = jax.nn.softmax(jnp.concatenate([s_loc, s_ctx], -1), axis=-1).astype(v.dtype)
        return (jnp.einsum('bhqn,bqnhd->bqhd', p[..., :nk], vg)
                + jnp.einsum('bhqs,bshd->bqhd', p[..., nk:], v_ctx))

    o = lax.map(row_block, (qr, idx, bias))
    return o.transpose(1, 0, 2, 3, 4).reshape(b, s_len, h, d)

def even_mixer(u_lat, u_ctx, need_ctx, w_in, w_out, conv_w, a_log, dt_bias, out_norm,
               q_norm, w_q_up, kv_norm, w_kv_up, rope):
    b, s_len, _ = u_lat.shape
    lat = split_cols(u_lat @ w_in, EVEN_SPLITS)
    ctx = split_cols(u_ctx @ w_in, EVEN_SPLITS)
    o_lat, o_ctx = gdn_bidirectional(gdn_prepare(lat[0], lat[2], lat[3], conv_w, a_log, dt_bias),
                                     gdn_prepare(ctx[0], ctx[2], ctx[3], conv_w, a_log, dt_bias))
    a_lat = gdn_output(o_lat, lat[1], out_norm)
    k_c, v_c = mla_kv(ctx[5], ctx[6], kv_norm, w_kv_up, None)
    k_l, v_l = mla_kv(lat[5], lat[6], kv_norm, w_kv_up, rope)
    q_l = mla_q(lat[4], q_norm, w_q_up, rope)
    scale = (MLA_NOPE + MLA_ROPE) ** -0.5
    b_lat = blocked_attention(q_l, jnp.concatenate([k_c, k_l], 1), jnp.concatenate([v_c, v_l], 1), scale)
    y_lat = jnp.concatenate([a_lat, b_lat.reshape(b, s_len, -1)], -1) @ w_out
    if not need_ctx:
        return y_lat, None
    l_len = u_ctx.shape[1]
    a_ctx = gdn_output(o_ctx, ctx[1], out_norm)
    b_ctx = blocked_attention(mla_q(ctx[4], q_norm, w_q_up, None), k_c, v_c, scale)
    y_ctx = jnp.concatenate([a_ctx, b_ctx.reshape(b, l_len, -1)], -1) @ w_out
    return y_lat, y_ctx

def odd_mixer(u_lat, u_ctx, need_ctx, w_in, w_out, rpb, q_norm, k_norm, rope):
    b, s_len, _ = u_lat.shape
    lat = split_cols(u_lat @ w_in, ODD_SPLITS)
    ctx = split_cols(u_ctx @ w_in, ODD_SPLITS)
    kn_c, vn_c = to_heads(ctx[1], NA_HEADS), to_heads(ctx[2], NA_HEADS)
    c_lat = neighbourhood_attention(to_heads(lat[0], NA_HEADS), to_heads(lat[1], NA_HEADS),
                                    to_heads(lat[2], NA_HEADS), kn_c, vn_c, rpb)
    kd_c = rms_norm(to_heads(ctx[4], GQA_KV_HEADS), k_norm)
    vd_c = to_heads(ctx[5], GQA_KV_HEADS)
    qd_l = apply_rope(rms_norm(to_heads(lat[3], GQA_HEADS), q_norm), *rope)
    kd_l = apply_rope(rms_norm(to_heads(lat[4], GQA_KV_HEADS), k_norm), *rope)
    scale = GQA_DIM ** -0.5
    d_lat = blocked_attention(qd_l, jnp.concatenate([kd_c, kd_l], 1),
                              jnp.concatenate([vd_c, to_heads(lat[5], GQA_KV_HEADS)], 1), scale)
    y_lat = jnp.concatenate([c_lat.reshape(b, s_len, -1), d_lat.reshape(b, s_len, -1)], -1) @ w_out
    if not need_ctx:
        return y_lat, None
    l_len = u_ctx.shape[1]
    c_ctx_o = blocked_attention(to_heads(ctx[0], NA_HEADS), kn_c, vn_c, NA_DIM ** -0.5)
    d_ctx = blocked_attention(rms_norm(to_heads(ctx[3], GQA_HEADS), q_norm), kd_c, vd_c, scale)
    y_ctx = jnp.concatenate([c_ctx_o.reshape(b, l_len, -1), d_ctx.reshape(b, l_len, -1)], -1) @ w_out
    return y_lat, y_ctx

def first_inputs(seed: int = 0) -> dict:
    key = jax.random.key(seed)
    ks = iter(jax.random.split(key, 40))
    f32 = jnp.float32

    def nrm(shape, scale):
        return jax.random.normal(next(ks), shape, f32) * scale

    def gain(shape):
        return 1.0 + 0.05 * jax.random.normal(next(ks), shape, f32)

    d = D_MODEL
    x = nrm((BATCH, SEQ, d), 1.0)
    c = nrm((BATCH, d), 1.0)
    ctx = nrm((BATCH, CTX_LEN, d), 1.0)
    c_ctx = nrm((d,), 1.0)
    w_mod = nrm((DEPTH, d, 6 * d), 0.5 * d ** -0.5)
    b_mod = nrm((DEPTH, 6 * d), 0.01)
    g_pre_mix = gain((DEPTH, d))
    g_post_mix = gain((DEPTH, d))
    g_pre_ffn = gain((DEPTH, d))
    g_post_ffn = gain((DEPTH, d))
    w_ffn_gate = nrm((DEPTH, d, D_FF), d ** -0.5)
    w_ffn_up = nrm((DEPTH, d, D_FF), d ** -0.5)
    w_ffn_down = nrm((DEPTH, D_FF, d), D_FF ** -0.5)
    w_in_even = nrm((N_EVEN, d, IN_EVEN), d ** -0.5)
    w_out_even = nrm((N_EVEN, MIX_EVEN, d), MIX_EVEN ** -0.5)
    gdn_conv = nrm((N_EVEN, GDN_CONV, 2 * GDN_QK_W + GDN_V_W), GDN_CONV ** -0.5)
    gdn_a_log = jnp.log(jax.random.uniform(next(ks), (N_EVEN, 2, GDN_HEADS), f32, 1.0, 16.0))
    dt = jnp.exp(jax.random.uniform(next(ks), (N_EVEN, 2, GDN_HEADS), f32,
                                    float(np.log(1e-3)), float(np.log(1e-1))))
    gdn_dt_bias = dt + jnp.log(-jnp.expm1(-dt))
    gdn_out_norm = gain((N_EVEN, GDN_DV))
    mla_q_norm = gain((N_EVEN, MLA_Q_LORA))
    mla_w_q_up = nrm((N_EVEN, MLA_Q_LORA, MLA_HEADS * (MLA_NOPE + MLA_ROPE)), MLA_Q_LORA ** -0.5)
    mla_kv_norm = gain((N_EVEN, MLA_KV_LORA))
    mla_w_kv_up = nrm((N_EVEN, MLA_KV_LORA, MLA_HEADS * (MLA_NOPE + MLA_V)), MLA_KV_LORA ** -0.5)
    w_in_odd = nrm((N_ODD, d, IN_ODD), d ** -0.5)
    w_out_odd = nrm((N_ODD, MIX_ODD, d), MIX_ODD ** -0.5)
    na_rpb = nrm((N_ODD, NA_HEADS, 2 * NA_WIN_H - 1, 2 * NA_WIN_W - 1), 0.1)
    gqa_q_norm = gain((N_ODD, GQA_DIM))
    gqa_k_norm = gain((N_ODD, GQA_DIM))
    return {'x': x, 'c': c, 'ctx': ctx, 'c_ctx': c_ctx, 'w_mod': w_mod, 'b_mod': b_mod,
            'g_pre_mix': g_pre_mix, 'g_post_mix': g_post_mix, 'g_pre_ffn': g_pre_ffn,
            'g_post_ffn': g_post_ffn, 'w_ffn_gate': w_ffn_gate, 'w_ffn_up': w_ffn_up,
            'w_ffn_down': w_ffn_down, 'w_in_even': w_in_even, 'w_out_even': w_out_even,
            'gdn_conv': gdn_conv, 'gdn_a_log': gdn_a_log, 'gdn_dt_bias': gdn_dt_bias,
            'gdn_out_norm': gdn_out_norm, 'mla_q_norm': mla_q_norm, 'mla_w_q_up': mla_w_q_up,
            'mla_kv_norm': mla_kv_norm, 'mla_w_kv_up': mla_w_kv_up, 'w_in_odd': w_in_odd,
            'w_out_odd': w_out_odd, 'na_rpb': na_rpb, 'gqa_q_norm': gqa_q_norm, 'gqa_k_norm': gqa_k_norm}

def first_block(x, c, ctx, c_ctx, w_mod, b_mod, g_pre_mix, g_post_mix, g_pre_ffn, g_post_ffn,
              w_ffn_gate, w_ffn_up, w_ffn_down, w_in_even, w_out_even, gdn_conv, gdn_a_log,
              gdn_dt_bias, gdn_out_norm, mla_q_norm, mla_w_q_up, mla_kv_norm, mla_w_kv_up,
              w_in_odd, w_out_odd, na_rpb, gqa_q_norm, gqa_k_norm):
    s_len = x.shape[1]
    rope_mla = axial_rope(s_len, MLA_ROPE)
    rope_gqa = axial_rope(s_len, GQA_DIM)
    h, hc = x, ctx
    for i in range(DEPTH):
        last = i == DEPTH - 1
        mod = (jax.nn.silu(c) @ w_mod[i] + b_mod[i])[:, None, :]
        mod_c = (jax.nn.silu(c_ctx) @ w_mod[i] + b_mod[i])[None, None, :]
        sh_m, sc_m, gt_m, sh_f, sc_f, gt_f = jnp.split(mod, 6, axis=-1)
        csh_m, csc_m, cgt_m, csh_f, csc_f, cgt_f = jnp.split(mod_c, 6, axis=-1)
        u = modulate(rms_norm(h, g_pre_mix[i]), sh_m, sc_m)
        uc = modulate(rms_norm(hc, g_pre_mix[i]), csh_m, csc_m)
        j = i // 2
        if i % 2 == 0:
            y, yc = even_mixer(u, uc, not last, w_in_even[j], w_out_even[j], gdn_conv[j], gdn_a_log[j],
                               gdn_dt_bias[j], gdn_out_norm[j], mla_q_norm[j], mla_w_q_up[j],
                               mla_kv_norm[j], mla_w_kv_up[j], rope_mla)
        else:
            y, yc = odd_mixer(u, uc, not last, w_in_odd[j], w_out_odd[j], na_rpb[j],
                              gqa_q_norm[j], gqa_k_norm[j], rope_gqa)
        h = h + gt_m * rms_norm(y, g_post_mix[i])
        f = swiglu(modulate(rms_norm(h, g_pre_ffn[i]), sh_f, sc_f), w_ffn_gate[i], w_ffn_up[i], w_ffn_down[i])
        h = h + gt_f * rms_norm(f, g_post_ffn[i])
        if not last:
            hc = hc + cgt_m * rms_norm(yc, g_post_mix[i])
            fc = swiglu(modulate(rms_norm(hc, g_pre_ffn[i]), csh_f, csc_f), w_ffn_gate[i], w_ffn_up[i], w_ffn_down[i])
            hc = hc + cgt_f * rms_norm(fc, g_post_ffn[i])
    return h


HEAD_DIM = 64
ATTN_WIDTH = D_MODEL // 2
ATTN_HEADS = ATTN_WIDTH // HEAD_DIM
KV_HEADS = 2
GROUP = ATTN_HEADS // KV_HEADS
IDX_HEADS = 16
IDX_DIM = 64
INDEX_TOPK = 256
CONV_WIDTH = D_MODEL // 4
CONV_KERNEL = 31
POOL_WIDTH = D_MODEL // 4
POOL_GROUPS = 4
POOL_GROUP_DIM = POOL_WIDTH // POOL_GROUPS
POOL_WINDOWS = (2, 4, 8, 16)
POOL_PAD = max(POOL_WINDOWS)
MIX_WIDTH = ATTN_WIDTH + CONV_WIDTH + POOL_WIDTH
D_FF_2 = 4 * D_MODEL
PLE_DIM = 256
ROPE_THETA_2 = 500000.0
ROPE_DIM = HEAD_DIM // 4
MAX_POS_OFFSET = 1024
LN_EPS = 1e-5

IN_SIZES = (
    ATTN_WIDTH,
    KV_HEADS * HEAD_DIM,
    KV_HEADS * HEAD_DIM,
    IDX_HEADS * IDX_DIM,
    IDX_DIM,
    IDX_HEADS,
    2 * CONV_WIDTH,
    POOL_WIDTH,
)
IN_WIDTH = int(sum(IN_SIZES))
IN_SPLITS = [int(v) for v in np.cumsum(IN_SIZES)[:-1]]


def rmsnorm(x, g):
    xf = x.astype(jnp.float32)
    y = xf * lax.rsqrt(jnp.mean(xf * xf, axis=-1, keepdims=True) + NORM_EPS)
    return (y * g.astype(jnp.float32)).astype(x.dtype)

def layernorm(x, g, b):
    xf = x.astype(jnp.float32)
    mu = jnp.mean(xf, axis=-1, keepdims=True)
    var = jnp.mean(jnp.square(xf - mu), axis=-1, keepdims=True)
    y = (xf - mu) * lax.rsqrt(var + LN_EPS)
    return (y * g.astype(jnp.float32) + b.astype(jnp.float32)).astype(x.dtype)

def rope_tables(positions):
    inv_freq = ROPE_THETA_2 ** (-jnp.arange(0, ROPE_DIM, 2, dtype=jnp.float32) / ROPE_DIM)
    ang = positions.astype(jnp.float32)[..., None] * inv_freq
    return jnp.cos(ang)[:, :, None, :], jnp.sin(ang)[:, :, None, :]

def partial_rope(x, cos, sin):
    half = ROPE_DIM // 2
    cos = cos.astype(x.dtype)
    sin = sin.astype(x.dtype)
    x1 = x[..., :half]
    x2 = x[..., half:ROPE_DIM]
    return jnp.concatenate([x1 * cos - x2 * sin, x2 * cos + x1 * sin, x[..., ROPE_DIM:]], axis=-1)

def dsa_sparse_attention(q, k, v, qi, ki, wi):
    B, S = q.shape[0], q.shape[1]
    n_blk = S // Q_BLOCK
    k_sel = min(INDEX_TOPK, S // 4)
    idx_scale = (IDX_DIM ** -0.5) * (IDX_HEADS ** -0.5)
    att_scale = HEAD_DIM ** -0.5
    neg = jnp.finfo(jnp.float32).min
    key_pos = jnp.arange(S)
    b_idx = jnp.arange(B)[:, None, None]
    ki_f = ki.astype(jnp.float32)

    def to_blocks(t):
        return jnp.moveaxis(t.reshape((B, n_blk, Q_BLOCK) + t.shape[2:]), 1, 0)

    q_b = to_blocks(q.reshape(B, S, KV_HEADS, GROUP, HEAD_DIM))
    qi_b = to_blocks(qi)
    wi_b = to_blocks(wi)
    t_b = key_pos.reshape(n_blk, Q_BLOCK)

    def block(args):
        q_blk, qi_blk, wi_blk, t_blk = args
        dots = jnp.einsum('bthd,bsd->bths', qi_blk.astype(jnp.float32), ki_f)
        idx = jnp.einsum('bths,bth->bts', jax.nn.relu(dots), wi_blk.astype(jnp.float32)) * idx_scale
        causal = key_pos[None, :] <= t_blk[:, None]
        idx = jnp.where(causal[None], idx, -jnp.inf)
        _, sel = lax.top_k(idx, k_sel)
        valid = sel <= t_blk[None, :, None]
        k_g = k[b_idx, sel]
        v_g = v[b_idx, sel]
        s = jnp.einsum('bthgd,btnhd->bthgn', q_blk, k_g).astype(jnp.float32) * att_scale
        s = jnp.where(valid[:, :, None, None, :], s, neg)
        pr = jax.nn.softmax(s, axis=-1).astype(v.dtype)
        o = jnp.einsum('bthgn,btnhd->bthgd', pr, v_g)
        return o.reshape(B, Q_BLOCK, ATTN_WIDTH)

    out = lax.map(block, (q_b, qi_b, wi_b, t_b))
    return jnp.moveaxis(out, 0, 1).reshape(B, S, ATTN_WIDTH)

def conformer_conv(u, conv_dw, conv_b, ln_g, ln_b, conv_pw):
    a, g = jnp.split(u, 2, axis=-1)
    y = a * jax.nn.sigmoid(g)
    y = lax.conv_general_dilated(
        y, conv_dw[:, None, :], window_strides=(1,), padding=[(CONV_KERNEL - 1, 0)],
        dimension_numbers=('NWC', 'WIO', 'NWC'), feature_group_count=CONV_WIDTH)
    y = y + conv_b
    y = jax.nn.silu(layernorm(y, ln_g, ln_b))
    return jnp.einsum('bsc,cd->bsd', y, conv_pw)

def multiscale_pool(u, pool_w, pool_scale):
    B, S, _ = u.shape
    uf = u.astype(jnp.float32)
    c = jnp.cumsum(uf, axis=1)
    c_pad = jnp.concatenate([jnp.zeros((B, POOL_PAD, POOL_WIDTH), jnp.float32), c], axis=1)
    t = jnp.arange(S)
    outs = []
    for gi, w in enumerate(POOL_WINDOWS):
        sl = slice(gi * POOL_GROUP_DIM, (gi + 1) * POOL_GROUP_DIM)
        win_sum = c[:, :, sl] - c_pad[:, POOL_PAD - w:POOL_PAD - w + S, sl]
        count = jnp.minimum(t + 1, w).astype(jnp.float32)[None, :, None]
        outs.append(win_sum / count - uf[:, :, sl])
    y = jnp.stack(outs, axis=2).astype(u.dtype)
    y = jnp.einsum('bsgc,gcd->bsgd', y, pool_w).reshape(B, S, POOL_WIDTH)
    return y * pool_scale

def second_inputs(seed: int = 0) -> dict:
    key = jax.random.key(seed)
    ks = jax.random.split(key, 24)
    nrm = jax.random.normal
    f32 = jnp.float32
    L = DEPTH
    x = nrm(ks[0], (BATCH, SEQ, D_MODEL), f32)
    p = nrm(ks[1], (DEPTH, BATCH, SEQ, PLE_DIM), f32)
    offs = jax.random.randint(ks[2], (BATCH, 1), 0, MAX_POS_OFFSET, dtype=jnp.int32)
    positions = (offs + jnp.arange(SEQ, dtype=jnp.int32)[None, :]).astype(jnp.int32)
    return {
        "x": x,
        "p": p,
        "positions": positions,
        "norm_mix_pre": 1.0 + 0.1 * nrm(ks[3], (L, D_MODEL), f32),
        "w_in": nrm(ks[4], (L, D_MODEL, IN_WIDTH), f32) * D_MODEL ** -0.5,
        "conv_dw": nrm(ks[5], (L, CONV_KERNEL, CONV_WIDTH), f32) * CONV_KERNEL ** -0.5,
        "conv_b": 0.02 * nrm(ks[6], (L, CONV_WIDTH), f32),
        "conv_ln_g": 1.0 + 0.1 * nrm(ks[7], (L, CONV_WIDTH), f32),
        "conv_ln_b": 0.02 * nrm(ks[8], (L, CONV_WIDTH), f32),
        "conv_pw": nrm(ks[9], (L, CONV_WIDTH, CONV_WIDTH), f32) * CONV_WIDTH ** -0.5,
        "pool_w": nrm(ks[10], (L, POOL_GROUPS, POOL_GROUP_DIM, POOL_GROUP_DIM), f32) * POOL_GROUP_DIM ** -0.5,
        "pool_scale": 1.0 + 0.1 * nrm(ks[11], (L, POOL_WIDTH), f32),
        "w_out": nrm(ks[12], (L, MIX_WIDTH, D_MODEL), f32) * MIX_WIDTH ** -0.5,
        "norm_mix_post": 1.0 + 0.1 * nrm(ks[13], (L, D_MODEL), f32),
        "norm_mlp_pre": 1.0 + 0.1 * nrm(ks[14], (L, D_MODEL), f32),
        "w_up": nrm(ks[15], (L, D_MODEL, D_FF_2), f32) * D_MODEL ** -0.5,
        "w_down": nrm(ks[16], (L, D_FF_2, D_MODEL), f32) * D_FF_2 ** -0.5,
        "norm_mlp_post": 1.0 + 0.1 * nrm(ks[17], (L, D_MODEL), f32),
        "ple_proj": nrm(ks[18], (L, PLE_DIM, D_MODEL), f32) * PLE_DIM ** -0.5,
        "ple_gate": nrm(ks[19], (L, D_MODEL, D_MODEL), f32) * D_MODEL ** -0.5,
    }

def second_block(x, p, positions, norm_mix_pre, w_in, conv_dw, conv_b, conv_ln_g, conv_ln_b,
              conv_pw, pool_w, pool_scale, w_out, norm_mix_post, norm_mlp_pre, w_up, w_down,
              norm_mlp_post, ple_proj, ple_gate):
    B, S, _ = x.shape
    cos, sin = rope_tables(positions)
    h = x
    for i in range(DEPTH):
        a = rmsnorm(h, norm_mix_pre[i])
        u = jnp.einsum('bsd,de->bse', a, w_in[i])
        q, k, v, qi, ki, wi, u_conv, u_pool = jnp.split(u, IN_SPLITS, axis=-1)
        q = partial_rope(q.reshape(B, S, ATTN_HEADS, HEAD_DIM), cos, sin)
        k = partial_rope(k.reshape(B, S, KV_HEADS, HEAD_DIM), cos, sin)
        v = v.reshape(B, S, KV_HEADS, HEAD_DIM)
        qi = partial_rope(qi.reshape(B, S, IDX_HEADS, IDX_DIM), cos, sin)
        ki = partial_rope(ki[:, :, None, :], cos, sin)[:, :, 0, :]
        y_attn = dsa_sparse_attention(q, k, v, qi, ki, wi)
        y_conv = conformer_conv(u_conv, conv_dw[i], conv_b[i], conv_ln_g[i],
                                conv_ln_b[i], conv_pw[i])
        y_pool = multiscale_pool(u_pool, pool_w[i], pool_scale[i])
        mix = jnp.concatenate([y_attn, y_conv, y_pool], axis=-1)
        mix = jnp.einsum('bse,ed->bsd', mix, w_out[i])
        h = h + rmsnorm(mix, norm_mix_post[i])
        m = rmsnorm(h, norm_mlp_pre[i])
        m = jnp.square(jax.nn.relu(jnp.einsum('bsd,df->bsf', m, w_up[i])))
        m = jnp.einsum('bsf,fd->bsd', m, w_down[i])
        h = h + rmsnorm(m, norm_mlp_post[i])
        gate = jax.nn.sigmoid(jnp.einsum('bsd,de->bse', h, ple_gate[i]))
        h = h + gate * jnp.einsum('bsp,pd->bsd', p[i], ple_proj[i])
    return h


def setup_inputs(seed=0):
    out = dict(first_inputs(seed))
    for name, value in second_inputs(seed + 1).items():
        if name != "x":
            out[name + "_2"] = value
    return out


def reference(
    x, c, ctx, c_ctx, w_mod, b_mod, g_pre_mix, g_post_mix, g_pre_ffn, g_post_ffn, w_ffn_gate,
    w_ffn_up, w_ffn_down, w_in_even, w_out_even, gdn_conv, gdn_a_log, gdn_dt_bias, gdn_out_norm,
    mla_q_norm, mla_w_q_up, mla_kv_norm, mla_w_kv_up, w_in_odd, w_out_odd, na_rpb, gqa_q_norm,
    gqa_k_norm, p_2, positions_2, norm_mix_pre_2, w_in_2, conv_dw_2, conv_b_2, conv_ln_g_2,
    conv_ln_b_2, conv_pw_2, pool_w_2, pool_scale_2, w_out_2, norm_mix_post_2, norm_mlp_pre_2,
    w_up_2, w_down_2, norm_mlp_post_2, ple_proj_2, ple_gate_2,
):
    x = first_block(
        x, c, ctx, c_ctx, w_mod, b_mod, g_pre_mix, g_post_mix, g_pre_ffn, g_post_ffn,
        w_ffn_gate, w_ffn_up, w_ffn_down, w_in_even, w_out_even, gdn_conv, gdn_a_log,
        gdn_dt_bias, gdn_out_norm, mla_q_norm, mla_w_q_up, mla_kv_norm, mla_w_kv_up, w_in_odd,
        w_out_odd, na_rpb, gqa_q_norm, gqa_k_norm,
    )
    return second_block(
        x, p_2, positions_2, norm_mix_pre_2, w_in_2, conv_dw_2, conv_b_2, conv_ln_g_2,
        conv_ln_b_2, conv_pw_2, pool_w_2, pool_scale_2, w_out_2, norm_mix_post_2,
        norm_mlp_pre_2, w_up_2, w_down_2, norm_mlp_post_2, ple_proj_2, ple_gate_2,
    )


_drawn_inputs = setup_inputs


def setup_inputs(seed=0):
    import zlib

    import numpy as np

    out = dict(_drawn_inputs(seed))
    spreads = {}
    factors = {'mla_q_norm': 4.703,
     'mla_kv_norm': 2.98,
     'na_rpb': 12.351,
     'gqa_q_norm': 4.458,
     'gqa_k_norm': 4.477,
     'conv_ln_b_2': 4.665,
     'gdn_out_norm': 2.921}
    for name, (base, spread) in spreads.items():
        noise = np.random.default_rng([zlib.crc32(name.encode()), seed]).standard_normal(out[name].shape)
        drawn = base * np.exp(spread * noise) if base else spread * noise
        out[name] = jnp.asarray(drawn.astype(out[name].dtype))
    for name, factor in factors.items():
        out[name] = (out[name] * factor).astype(out[name].dtype)
    return out
```

```python
from contextlib import ExitStack

import concourse.bass as bass
from concourse import mybir
import numpy as np

F32 = mybir.dt.float32
I32 = mybir.dt.int32
ALU = mybir.AluOpType
ACT = mybir.ActivationFunctionType
AX = mybir.AxisListType.X

P = 128
D = 1024
KT = D // P
S = 256
T2 = 2 * S
GRID = 64
FF = 2816
FF2 = 4096
NEG = -1.0e30
TAKEN = -3.0e38
CHUNK = 64
HEADS = 8
TOPK = S // 4
CB = 16
RING = 5
EPS = 1e-6
LN_EPS = 1e-5
CONV = 31



def columns(width, start=0):
    return [list(range(start + P * i, start + P * (i + 1))) for i in range(width // P)]


EVEN_ODD = [0, 2, 4, 6, 1, 3, 5, 7]


def even_in_columns():
    ab = [[2048 + 8 * i + h for i in range(4) for h in EVEN_ODD] + [-1] * 32 + list(range(2464, 2496)) + [-1] * 32]
    return columns(2048) + ab + columns(256, 2080) + columns(128, 2336)


def paired(start):
    return [list(range(start + 64 * i, start + 64 * i + 64)) + list(range(start + 64 * (i + 4), start + 64 * (i + 4) + 64))
            for i in range(4)]


def pack_tiles(w, tiles, rows=None):
    rows = np.arange(w.shape[0]) if rows is None else rows
    out = []
    for t in tiles:
        t = np.array(t)
        b = np.zeros((len(rows), P), np.float32)
        b[:, t >= 0] = w[rows][:, t[t >= 0]]
        out.append(b.reshape(-1, P, P))
    return np.concatenate(out)


def pack_rows(w, tiles):
    b = pack_tiles(w, tiles)
    n = len(tiles)
    return np.ascontiguousarray(b.reshape(n, -1, P, P).transpose(1, 0, 2, 3)).reshape(-1, P, P)


def interleaved(a, b, k):
    return np.concatenate([a.reshape(-1, 1, k, P, P), b.reshape(-1, 1, k, P, P)], 1).reshape(-1, P, P)


def weight_blocks(x):
    out = []
    mods = [pack_rows(x["w_mod"][i], columns(512, 512 * n)) for i in range(2) for n in range(12)]
    out += mods[:4]
    out.append(pack_tiles(x["w_in_even"][0], even_in_columns()))
    out += mods[4:]
    kv = x["mla_w_kv_up"][0]
    out.append(pack_tiles(x["mla_w_q_up"][0], [list(range(96 * h, 96 * h + 96)) + [-1] * 32 for h in range(HEADS)]))
    out.append(pack_tiles(kv, [[128 * h + i for h in (2 * j, 2 * j + 1) for i in range(64)] for j in range(4)]))
    out.append(pack_tiles(kv, [[128 * h + 64 + i for h in (2 * j, 2 * j + 1) for i in range(64)] for j in range(4)]))
    out.append(pack_tiles(x["w_out_even"][0], columns(D)))
    for i in range(2):
        if i == 1:
            w = x["w_in_odd"][0]
            out.append(pack_tiles(w, columns(512)))
            out.append(pack_tiles(w, paired(1536)))
            out.append(pack_tiles(w, columns(512, 512)))
            out.append(pack_tiles(w, columns(128, 2048)))
            out.append(pack_rows(w, columns(512, 1024)))
            out.append(pack_rows(w, columns(128, 2176)))
            rows = np.concatenate([np.arange(512)] + [np.array(t) for t in paired(512)])
            out.append(pack_tiles(x["w_out_odd"][0], columns(D), rows))
        out.append(interleaved(pack_tiles(x["w_ffn_gate"][i], columns(FF)), pack_tiles(x["w_ffn_up"][i], columns(FF)), KT))
        out.append(pack_tiles(x["w_ffn_down"][i], columns(D)))
    for i in range(2):
        w = x["w_in_2"][i]
        o = [0, 512, 640, 768, 1792, 1856, 1872, 2384]
        out.append(pack_tiles(w, columns(512, o[6])))
        out.append(pack_tiles(w, columns(256, o[7])))
        out.append(pack_tiles(w, paired(0)))
        out.append(pack_tiles(w, columns(128, o[1])))
        out.append(pack_tiles(w, columns(1024, o[3])))
        out.append(pack_tiles(w, [list(range(o[4], o[4] + 64)) * 2]))
        out.append(pack_rows(w, columns(128, o[2])))
        out.append(pack_rows(w, [list(range(o[5], o[5] + 16)) + [-1] * 112]))
        out.append(pack_tiles(x["conv_pw_2"][i], columns(256)))
        pool = np.zeros((256, 256), np.float32)
        for g in range(4):
            pool[64 * g:64 * g + 64, 64 * g:64 * g + 64] = x["pool_w_2"][i, g]
        out.append(np.stack([pool[:P, :P], pool[P:, P:]]))
        rows = np.concatenate([np.array(t) for t in paired(0)] + [np.arange(512, 1024)])
        out.append(pack_tiles(x["w_out_2"][i], columns(D), rows))
        out.append(pack_tiles(x["w_up_2"][i], columns(FF2)))
        out.append(pack_tiles(x["w_down_2"][i], columns(D)))
        out.append(pack_tiles(x["ple_gate_2"][i], columns(D)))
        out.append(pack_tiles(x["ple_proj_2"][i], columns(D)))
    return out




def rotation(width, dims, start):
    r = np.zeros((P, P), np.float32)
    for b in range(0, P, width):
        for j in range(dims // 2):
            if b + start + dims <= P:
                r[b + start + dims // 2 + j, b + start + j] = -1.0
                r[b + start + j, b + start + dims // 2 + j] = 1.0
    return r


def axial(dims, theta=10000.0):
    t = np.arange(S)
    n = dims // 4
    inv = (np.float32(theta) ** (-np.arange(n, dtype=np.float32) / np.float32(n))).astype(np.float32)
    ang = np.concatenate([(t // GRID).astype(np.float32)[:, None] * inv, (t % GRID).astype(np.float32)[:, None] * inv], -1)
    return np.cos(ang).T.astype(np.float32), np.sin(ang).T.astype(np.float32)


def constant_parts():
    c = {}
    i, j = np.arange(P)[:, None], np.arange(P)[None, :]
    same = (i // CHUNK) == (j // CHUNK)
    c["ones"] = np.ones((P, P))
    c["ident"] = (i == j)
    c["mirror"] = same & (i % CHUNK == CHUNK - 1 - j % CHUNK)
    c["halves"] = same
    c["upto"] = np.stack([same & (i <= j), same & (i >= j)], 1)
    c["chunk"] = np.stack([np.broadcast_to(i // CHUNK == n, (P, P)) for n in range(2)], 1)
    levels = []
    for d in range(2):
        for lv in range(6):
            b = 1 << lv
            lo, hi = (i, j) if d == 0 else (j, i)
            levels.append((i // (2 * b) == j // (2 * b)) & (lo % (2 * b) < b) & (hi % (2 * b) >= b))
    c["levels"] = np.stack(levels, 1)
    c["rot_mla"] = rotation(P, 32, 64)
    c["rot_gqa"] = rotation(64, 64, 0)
    c["rot_dsa"] = rotation(64, 16, 0)
    cs, sn = axial(32)
    c["mla_cos"], c["mla_sin"] = np.ones((P, S)), np.zeros((P, S))
    c["mla_cos"][64:96], c["mla_sin"][64:96] = np.concatenate([cs] * 2), np.concatenate([sn] * 2)
    cs, sn = axial(64)
    c["gqa_cos"], c["gqa_sin"] = np.concatenate([cs] * 4), np.concatenate([sn] * 4)
    inv = (np.float32(500000.0) ** (-np.arange(0, 16, 2, dtype=np.float32) / np.float32(16))).astype(np.float32)
    f = np.zeros((P, 1))
    for b in (0, 8, 64, 72):
        f[b:b + 8, 0] = inv
    c["dsa_freq"] = f
    t = np.arange(S)
    w = np.array([2, 4, 8, 16])
    c["pool_count"] = np.stack([1.0 / np.minimum(t + 1, w[2 * n + (np.arange(P) // 64)][:, None]) for n in range(2)], 1)
    q = np.arange(P)[:, None]
    c["causal"] = np.stack([np.where(t[None, :] <= q + P * n, 0.0, NEG) for n in range(2)], 1)
    col, kc = GRID - 1 - (q % GRID), np.arange(GRID)[None, :]
    start = np.clip(col - 8, 0, GRID - 16)
    inside = (kc >= start) & (kc < start + 16)
    c["window"] = inside
    c["outside"] = np.where(inside, 0.0, NEG)
    c["half_pi"] = np.full((P, 1), np.pi / 2)
    c["eps"] = np.full((P, 1), EPS)
    c["ln_eps"] = np.full((P, 1), LN_EPS)
    return {k: np.ascontiguousarray(np.asarray(v, np.float32).reshape(P, -1)) for k, v in c.items()}


def layout(sizes):
    at, out = 0, {}
    for name, n in sizes.items():
        out[name] = (at, n)
        at += n
    return out, at


VECTOR_SIZES = {
    "cond": 16, "b_mod": 96, "g_pre_mix": 16, "g_post_mix": 16, "g_pre_ffn": 16, "g_post_ffn": 16,
    "gdn_conv": 60, "gdn_out_norm": 1, "mla_q_norm": 2, "mla_kv_norm": 1, "gqa_q_norm": 1, "gqa_k_norm": 1,
    "norm_mix_pre": 16, "conv_dw": 2 * 2 * CONV, "conv_b": 4, "conv_ln_g": 4, "conv_ln_b": 4, "pool_scale": 4,
    "norm_mix_post": 16, "norm_mlp_pre": 16, "norm_mlp_post": 16,
}


def vector_parts(x):
    def cols(a):
        return np.ascontiguousarray(np.moveaxis(a.reshape(a.shape[:-1] + (-1, P)), -1, 0)).reshape(P, -1)

    def twice(a):
        return np.concatenate([a.reshape(-1, 1)] * 2)

    v = {
        "cond": np.ascontiguousarray(np.stack([x["c_ctx"], x["c"][0]], 0).reshape(2, KT, P).transpose(2, 1, 0)).reshape(P, -1),
        "gdn_conv": np.ascontiguousarray(x["gdn_conv"][0].reshape(5, 12, P).transpose(2, 1, 0)).reshape(P, -1),
        "gdn_out_norm": twice(x["gdn_out_norm"][0]), "gqa_q_norm": twice(x["gqa_q_norm"][0]),
        "gqa_k_norm": twice(x["gqa_k_norm"][0]), "mla_q_norm": cols(x["mla_q_norm"][0]),
        "mla_kv_norm": cols(x["mla_kv_norm"][0]),
        "conv_dw": np.ascontiguousarray(x["conv_dw_2"].reshape(2, CONV, 2, P).transpose(3, 0, 2, 1)).reshape(P, -1),
    }
    for n in ("b_mod", "g_pre_mix", "g_post_mix", "g_pre_ffn", "g_post_ffn"):
        v[n] = cols(x[n])
    for n in ("norm_mix_pre", "conv_b", "conv_ln_g", "conv_ln_b", "pool_scale", "norm_mix_post", "norm_mlp_pre", "norm_mlp_post"):
        v[n] = cols(x[n + "_2"])
    return v


class Counter:

    def __init__(self, sem):
        self.sem, self.n = sem, 0

    def reserve(self, k):
        b = self.n
        self.n += k
        return b


def need(eng, deps):
    for sig, count in deps:
        if count > 0:
            eng.wait_ge(sig.sem, count)


class Plan:

    ENGINES = ("sync", "gpsimd", "scalar", "vector", "tensor")

    def __init__(self, nc, ctx, const_at, vector_at, n_blocks):
        self.nc, self.ctx, self.const_at, self.vector_at = nc, ctx, const_at, vector_at
        self.n_chunks = -(-n_blocks // CB)
        self.programs = []
        self.counters = {}
        self.free = 0
        self.const = self.sbuf("constants", sum(n for _, n in const_at.values()))
        self.vec = self.sbuf("vector_params", sum(n for _, n in vector_at.values()))
        self.ring = self.sbuf("weight_ring", RING * CB * P).rearrange("p (r n) -> p r n", r=RING)
        self.psum = ctx.enter_context(nc.psum_tensor("banks", [P, 8, 512], F32))
        self.chunk_arrived = [self.counter(f"chunk_arrived_{i}") for i in range(RING)]
        self.taken = 0
        self.seen_chunk = -1
        self.last_use = {}
        self.steps = {"vector": self.counter("vector_order"), "scalar": self.counter("scalar_order")}

    def sbuf(self, name, n, dt=F32):
        return self.ctx.enter_context(self.nc.sbuf_tensor(name, [P, n], dt))[:, :]

    def counter(self, name):
        if name not in self.counters:
            self.counters[name] = Counter(self.ctx.enter_context(self.nc.semaphore(name)))
        return self.counters[name]

    def c(self, name):
        at, n = self.const_at[name]
        return self.const[:, at:at + n]

    def v(self, name):
        at, n = self.vector_at[name]
        return self.vec[:, at:at + n]

    def bank(self, n, width=512):
        return self.psum[:, n, 0:width]


    def next_blocks(self, n, done):
        first = self.taken
        self.taken += n
        for c in range(first // CB, self.taken // CB + 1):
            self.last_use[c] = done
        return first

    def block(self, i, n=1):
        return self.ring[:, i // CB % RING, i % CB * P:(i % CB + n) * P]

    def arrived(self, pe, i):
        c = i // CB
        if c > self.seen_chunk:
            pe.wait_ge(self.chunk_arrived[c % RING].sem, 16 * (c // RING + 1))
            self.seen_chunk = c

    def add(self, **programs):
        self.programs.append(programs)

    def in_turn(self, eng, name):
        sig = self.steps[name]

        def step(ins):
            sig.n += 1
            ins.then_inc(sig.sem, 1)
            eng.wait_ge(sig.sem, sig.n)
            return ins
        return step


def matmul_stage(K, n_m, n_k, rhs, T, evac, deps, who=None, k_ready=None, rows=None, banks=(0, 1, 2, 3), squares=False):
    who = who or (lambda m: "scalar")
    made, out = K.counter("products"), {e: K.counter(f"taken_out_by_{e}") for e in ("scalar", "vector")}
    b = made.reserve(n_m)
    after = []
    for m in range(n_m):
        e = out[who(m)]
        after.append((e, e.reserve(1) + 1))
    first = [K.next_blocks(n_k, (made, b + m + 1)) for m in range(n_m)]
    nb = len(banks)
    added = K.counter("squares_added")
    sb = added.reserve(n_m - 1) if squares else 0
    scalar_out = out["scalar"]

    def sum_squares(dve):
        for m in range(1, n_m):
            dve.wait_ge(scalar_out.sem, after[m][1])
            if m > 1:
                dve.wait_ge(added.sem, sb + m - 1)
            dve.tensor_tensor(out=K.sums[:, 0:T], in0=K.sums[:, 0:T], in1=K.square[:, m % 2, 0:T], op=ALU.add).then_inc(added.sem, 1)

    def square(act, m, ps):
        if m >= 3:
            act.wait_ge(added.sem, sb + m - 2)
        return act.activation(K.square[:, m % 2, 0:T] if m else K.sums[:, 0:T], ps, ACT.Square)

    def tensor(pe):
        need(pe, deps)
        for m in range(n_m):
            if m >= nb:
                need(pe, [after[m - nb]])
            lo, hi = rows(m) if rows else (0, P)
            for k in range(n_k):
                if m == 0 and k_ready:
                    need(pe, k_ready(k))
                K.arrived(pe, first[m] + k)
                mm = pe.matmul(K.psum[lo:hi, banks[m % nb], 0:T], K.block(first[m] + k)[:, lo:hi], rhs(k), start=(k == 0), stop=(k == n_k - 1))
            mm.then_inc(made.sem, 1)

    def taker(mine):
        def program(eng):
            for m in range(n_m):
                if who(m) == mine:
                    lo, hi = rows(m) if rows else (0, P)
                    eng.wait_ge(made.sem, b + m + 1)
                    ins = evac(eng, m, K.psum[lo:hi, banks[m % nb], 0:T])
                    if squares:
                        ins = square(eng, m, K.psum[lo:hi, banks[m % nb], 0:T])
                    ins.then_inc(out[mine].sem, 1)
        return program

    K.add(tensor=tensor, scalar=taker("scalar"), vector=sum_squares if squares else taker("vector"))
    if squares:
        return [after[-1], (added, sb + n_m - 1)]
    last = {}
    for sig, count in after:
        last[sig.sem.name if hasattr(sig.sem, "name") else id(sig)] = (sig, count)
    return list(last.values())


def token_stage(K, n_k, width, lhs, n_t, evac, deps, banks=(0, 1, 2, 3)):
    made, out = K.counter("products"), K.counter("taken_out_by_scalar")
    b, e = made.reserve(1), out.reserve(n_t)
    n = -(-width // P)
    first = K.next_blocks(n_k * n, (made, b + 1))

    def tensor(pe):
        need(pe, deps)
        for k in range(n_k):
            K.arrived(pe, first + k * n)
            for t in range(n_t):
                mm = pe.matmul(K.bank(banks[t], width), lhs(k, t), K.block(first + k * n, n)[:, 0:width], start=(k == 0), stop=(k == n_k - 1))
        mm.then_inc(made.sem, 1)

    def scalar(act):
        act.wait_ge(made.sem, b + 1)
        for t in range(n_t):
            evac(act, t, K.bank(banks[t], width)).then_inc(out.sem, 1)

    K.add(tensor=tensor, scalar=scalar)
    return [(out, e + n_t)]


def scale_stage(K, groups, T, lhs, scale, apply, deps, eps="eps", n_apply=None, src_ready=None, sums=None):
    squared, summed, rooted, applied = (K.counter(n) for n in ("squared", "summed", "rooted", "applied"))
    n = 1 if sums is not None else sum(len(g) for g in groups)
    sq, su, ro = squared.reserve(n if sums is None else 0), summed.reserve(n), rooted.reserve(len(groups))
    ap = applied.reserve(n_apply or len(groups))

    def scalar(act):
        need(act, deps)
        i = 0 if sums is None else 1
        for g, tiles in enumerate(groups):
            for t, src in enumerate(tiles if sums is None else []):
                if src_ready:
                    need(act, src_ready(t))
                if i >= K.n_square:
                    act.wait_ge(summed.sem, su + i - K.n_square + 1)
                act.activation(K.square[:, i % K.n_square, 0:T], src, ACT.Square).then_inc(squared.sem, 1)
                i += 1
            act.wait_ge(summed.sem, su + i)
            if g >= 2:
                act.wait_ge(applied.sem, ap + (g - 1) * (n_apply or len(groups)) // len(groups))
            act.activation(K.root[:, g % 2, 0:T], K.bank(4 + g % 2, T), ACT.Sqrt, bias=K.c(eps), scale=scale).then_inc(rooted.sem, 1)

    def tensor(pe):
        if sums is not None:
            need(pe, deps)
            pe.matmul(K.bank(4, T), lhs, sums, start=True, stop=True).then_inc(summed.sem, 1)
            return
        i = 0
        for g, tiles in enumerate(groups):
            if g >= 2:
                pe.wait_ge(rooted.sem, ro + g - 1)
            for t in range(len(tiles)):
                pe.wait_ge(squared.sem, sq + i + 1)
                pe.matmul(K.bank(4 + g % 2, T), lhs, K.square[:, i % K.n_square, 0:T], start=(t == 0), stop=(t == len(tiles) - 1)).then_inc(summed.sem, 1)
                i += 1

    def vector(dve):
        step = K.in_turn(dve, "vector")
        for g in range(len(groups)):
            dve.wait_ge(rooted.sem, ro + g + 1)
            r = K.inverse[:, g % 2, 0:T]
            step(dve.reciprocal(r, K.root[:, g % 2, 0:T]))
            apply(dve, g, r, lambda ins: ins.then_inc(applied.sem, 1))

    K.add(scalar=scalar, tensor=tensor, vector=vector)
    return applied, ap, [(applied, ap + (n_apply or len(groups)))]


def modulated_norm(K, h, T, lo, gain, shift, out, deps, src_ready=None):
    shifted = K.counter("shifted")
    b = shifted.reserve(KT)
    halves = range(lo // S, 2) if T == T2 or lo else range(2)

    def apply(dve, g, r, emit):
        for k in range(KT):
            for hf in halves:
                o = hf * S - lo
                ins = dve.scalar_tensor_tensor(out=out[:, k, o:o + S], in0=h[:, k, hf * S:hf * S + S], scalar=gain(k, hf), in1=r[:, o:o + S], op0=ALU.mult, op1=ALU.mult)
            emit(ins)

    applied, ap, ready = scale_stage(K, [[h[:, k, lo:lo + T] for k in range(KT)]], T, K.c("ones"), 1.0 / D, apply, deps, n_apply=KT, src_ready=src_ready)
    if shift is None:
        return (lambda k: [(applied, ap + k + 1)]), ready

    def scalar(act):
        for k in range(KT):
            act.wait_ge(applied.sem, ap + k + 1)
            for hf in halves:
                o = hf * S - lo
                ins = act.activation(out[:, k, o:o + S], out[:, k, o:o + S], ACT.Identity, bias=shift(k, hf))
            ins.then_inc(shifted.sem, 1)

    K.add(scalar=scalar)
    return (lambda k: [(shifted, b + k + 1)]), [(shifted, b + KT)]


def residual(K, h, T, lo, y, gain, deps):
    halves = range(lo // S, 2)

    def apply(dve, g, r, emit):
        marks = K.steps["vector"]
        for k in range(KT + 1):
            if k < KT:
                for hf in halves:
                    o = hf * S - lo
                    ins = dve.scalar_tensor_tensor(out=y[:, k, o:o + S], in0=y[:, k, o:o + S], scalar=gain(k, hf), in1=r[:, o:o + S], op0=ALU.mult, op1=ALU.mult)
                ins.then_inc(marks.sem, 1)
                marks.n += 1
            if k:
                dve.wait_ge(marks.sem, marks.n - (k < KT))
                emit(dve.tensor_tensor(out=h[:, k - 1, lo:lo + T], in0=h[:, k - 1, lo:lo + T], in1=y[:, k - 1, 0:T], op=ALU.add))

    applied, ap, ready = scale_stage(K, [[y[:, k, 0:T] for k in range(KT)]], T, K.c("ones"), 1.0 / D, apply, deps, n_apply=KT, sums=K.sums[:, 0:T])
    return ready, lambda k: [(applied, ap + k + 1)]


class Modulation:

    def __init__(self, K, layer, n, silu, mod, product_bank, turned_bank):
        self.K, self.layer, self.n, self.silu, self.mod = K, layer, n, silu, mod
        self.banks = product_bank, turned_bank
        self.sig = [K.counter(x) for x in ("mod_product", "mod_kept", "mod_turned", "mod_added")]
        self.at = [x.reserve(1) for x in self.sig]
        self.first = K.next_blocks(4 * KT, (self.sig[0], self.at[0] + 1))
        self.row = K.root[:, self.at[0] % 2, :]

    def after(self, i):
        return [(self.sig[i], self.at[i] + 1)]

    def product(self, pe):
        need(pe, self.K.silu_ready)
        for k in range(KT):
            self.K.arrived(pe, self.first + 4 * k)
            mm = pe.matmul(self.K.bank(self.banks[0]), self.silu[:, k, :], self.K.block(self.first + 4 * k, 4), start=(k == 0), stop=(k == KT - 1))
        mm.then_inc(self.sig[0].sem, 1)

    def keep(self, act):
        if self.at[2] >= 2:
            act.wait_ge(self.sig[2].sem, self.at[2] - 1)
        need(act, self.after(0))
        act.activation(self.row, self.K.bank(self.banks[0]), ACT.Copy).then_inc(self.sig[1].sem, 1)

    def turn(self, pe):
        need(pe, self.after(1))
        for j in range(4):
            mm = pe.transpose(self.K.bank(self.banks[1])[:, j * P:j * P + P], self.row[:, j * P:j * P + P], self.K.c("ident"))
        mm.then_inc(self.sig[2].sem, 1)

    def add(self, dve):
        need(dve, self.after(2))
        bias = self.K.v("b_mod").rearrange("p (l m) -> p l m", l=2)[:, self.layer, 4 * self.n:4 * self.n + 4]
        two = self.K.bank(self.banks[1]).rearrange("p (j c x) -> p j c x", j=4, c=2)[:, :, :, 0]
        dve.tensor_tensor(out=self.mod[:, self.layer, 4 * self.n:4 * self.n + 4, :], in0=two, in1=bc(bias, 2, 2), op=ALU.add).then_inc(self.sig[3].sem, 1)


def modulation_stage(K, chunks):
    def tensor(pe):
        for i, c in enumerate(chunks):
            if i >= 2:
                need(pe, chunks[i - 2].after(1))
            c.product(pe)
            if i:
                if i >= 3:
                    need(pe, chunks[i - 3].after(3))
                if i == 1:
                    need(pe, K.inputs_ready)
                chunks[i - 1].turn(pe)
        need(pe, chunks[-3].after(3))
        chunks[-1].turn(pe)

    def scalar(act):
        for c in chunks:
            c.keep(act)

    def vector(dve):
        for c in chunks:
            c.add(dve)
    K.add(tensor=tensor, scalar=scalar, vector=vector)
    return chunks[-1].after(3)


def gain_stage(K, deps, todo):
    sig = K.counter("gains")
    b = sig.reserve(1)

    def vector(dve):
        need(dve, deps)
        todo(dve, K.in_turn(dve, "vector")).then_inc(sig.sem, 1)

    K.add(vector=vector)
    return [(sig, b + 1)]


def attention_stage(K, units, length, n_q, scale, q, k, values, bias, out, deps, buf, place="ident"):
    nk = length // P
    scored, maxed, probed, turned, turned_out, weighed, normed = (K.counter(n) for n in ("scores", "maxima", "probabilities", "turned", "turned_out", "weighed", "normalised"))
    n = units * n_q
    sc, mx, pr, tu, to = (s.reserve(n) for s in (scored, maxed, probed, turned, turned_out))
    we, no = weighed.reserve(units), normed.reserve(units)
    prob, probT, small, rec = buf

    def tensor(pe):
        need(pe, deps)

        def score(i):
            u, t = divmod(i, n_q)
            if i >= 2:
                pe.wait_ge(probed.sem, pr + i - 1)
            ps = K.bank(i % 2, length)
            b = bias(u, t) if bias else None
            mm = pe.matmul(ps, q(u, t), k(u), start=True, stop=b is None)
            if b is not None:
                w = b.shape[-1]
                mm = pe.matmul(ps[:, length - w:length], K.c(place), b, start=False, stop=True)
            mm.then_inc(scored.sem, 1)

        def turn(i):
            pe.wait_ge(probed.sem, pr + i + 1)
            if i >= 2:
                pe.wait_ge(turned_out.sem, to + i - 1)
            for kt in range(nk):
                mm = pe.transpose(K.bank(2 + i % 2)[:, kt * P:kt * P + P], prob[:, i % 2, kt * P:kt * P + P], K.c("ident"))
            mm.then_inc(turned.sem, 1)

        def weigh(u):
            pe.wait_ge(turned_out.sem, to + (u + 1) * n_q)
            if u >= 2:
                pe.wait_ge(normed.sem, no + u - 1)
            for kt in range(nk):
                mm = pe.matmul(K.bank(4 + u % 2, n_q * P), values(u, kt), probT[:, u % 2, kt, 0:n_q * P], start=(kt == 0), stop=(kt == nk - 1))
            mm.then_inc(weighed.sem, 1)

        for i in range(n + 3):
            if i < n:
                score(i)
            if 1 <= i <= n:
                turn(i - 1)
            if i >= 3 and (i - 3) % n_q == n_q - 1:
                weigh((i - 3) // n_q)

    def scalar(act):
        for i in range(n + 1):
            if i < n:
                act.wait_ge(maxed.sem, mx + i + 1)
                if i >= 2:
                    act.wait_ge(turned.sem, tu + i - 1)
                act.activation(prob[:, i % 2, 0:length], K.bank(i % 2, length), ACT.Exp, bias=small[:, 2 + i % 2:3 + i % 2], scale=scale).then_inc(probed.sem, 1)
            if i >= 1:
                j = i - 1
                u, t = divmod(j, n_q)
                act.wait_ge(turned.sem, tu + j + 1)
                if u >= 2 and t == 0:
                    act.wait_ge(weighed.sem, we + u - 1)
                act.activation(probT[:, u % 2, 0:nk, t * P:t * P + P], K.bank(2 + j % 2, length).rearrange("p (k n) -> p k n", k=nk), ACT.Copy).then_inc(turned_out.sem, 1)

    def vector(dve):
        step = K.in_turn(dve, "vector")

        def normalise(u):
            dve.wait_ge(weighed.sem, we + u + 1)
            p = 64 * (u % 2)
            ps = K.bank(4 + u % 2, n_q * P)
            step(dve.reciprocal(rec[p:p + 64, 0:n_q * P], ps[64 - p:128 - p, :]))
            dve.tensor_tensor(out=out(u), in0=ps[p:p + 64, :], in1=rec[p:p + 64, 0:n_q * P], op=ALU.mult).then_inc(normed.sem, 1)

        for i in range(n + 4):
            if i < n:
                dve.wait_ge(scored.sem, sc + i + 1)
                if i >= 2:
                    dve.wait_ge(probed.sem, pr + i - 1)
                step(dve.reduce_max(small[:, i % 2:i % 2 + 1], K.bank(i % 2, length), AX))
                dve.tensor_scalar(small[:, 2 + i % 2:3 + i % 2], small[:, i % 2:i % 2 + 1], -scale, None, ALU.mult).then_inc(maxed.sem, 1)
            if i >= 4 and (i - 4) % n_q == n_q - 1:
                normalise((i - 4) // n_q)

    K.add(tensor=tensor, scalar=scalar, vector=vector)
    return [(normed, no + units)]


def rope_stage(K, items, rot, T, deps, tmp):
    turned, done = K.counter("rotated"), K.counter("roped")
    n = len(items)
    b, e = turned.reserve(n), done.reserve(n)

    def tensor(pe):
        need(pe, deps)
        for i, (x, lo, hi, *_) in enumerate(items):
            if i >= 2:
                pe.wait_ge(done.sem, e + i - 1)
            pe.matmul(K.psum[lo:hi, 4 + i % 2, 0:T], rot[lo:hi, lo:hi], x, start=True, stop=True).then_inc(turned.sem, 1)

    def vector(dve):
        step = K.in_turn(dve, "vector")
        need(dve, deps)
        for i, (x, lo, hi, cos, sin, out) in enumerate(items):
            dve.wait_ge(turned.sem, b + i + 1)
            dve.tensor_tensor(out=tmp[lo:hi, 0, 0:T], in0=K.psum[lo:hi, 4 + i % 2, 0:T], in1=sin, op=ALU.mult)
            step(dve.tensor_tensor(out=tmp[lo:hi, 1, 0:T], in0=x, in1=cos, op=ALU.mult))
            ins = dve.tensor_tensor(out=out, in0=tmp[lo:hi, 0, 0:T], in1=tmp[lo:hi, 1, 0:T], op=ALU.add)
            ins.then_inc(done.sem, 1)
            if i < n - 1:
                dve.wait_ge(done.sem, e + i + 1)

    K.add(tensor=tensor, vector=vector)
    return [(done, e + n)]


def feed_forward(K, u, T, n_f, hidden, tmp, y, deps, k_ready, meanwhile=None):
    made, gated, mixed = K.counter("pairs"), K.counter("gated"), K.counter("hidden")
    b, g, h = made.reserve(2 * n_f), gated.reserve(n_f), mixed.reserve(n_f)
    first = []
    for f in range(n_f):
        first += [K.next_blocks(KT, (made, b + 2 * f + 1)), K.next_blocks(KT, (made, b + 2 * f + 2))]

    def tensor(pe):
        need(pe, deps)
        for i in range(2 * n_f):
            if i >= 4:
                pe.wait_ge(mixed.sem, h + i // 2 - 1)
            for k in range(KT):
                if i == 0:
                    need(pe, k_ready(k))
                K.arrived(pe, first[i] + k)
                mm = pe.matmul(K.bank(i % 4, T), K.block(first[i] + k), u[:, k, 0:T], start=(k == 0), stop=(k == KT - 1))
            mm.then_inc(made.sem, 1)

    def scalar(act):
        for f in range(n_f):
            act.wait_ge(made.sem, b + 2 * f + 1)
            if f >= 2:
                act.wait_ge(mixed.sem, h + f - 1)
            act.activation(tmp[:, f % 2, 0:T], K.bank(2 * f % 4, T), ACT.Silu).then_inc(gated.sem, 1)

    def vector(dve):
        for f in range(n_f):
            dve.wait_ge(gated.sem, g + f + 1)
            dve.wait_ge(made.sem, b + 2 * f + 2)
            dve.tensor_tensor(out=hidden[:, f, 0:T], in0=K.bank((2 * f + 1) % 4, T), in1=tmp[:, f % 2, 0:T], op=ALU.mult).then_inc(mixed.sem, 1)

    K.add(tensor=tensor, scalar=scalar, vector=vector)
    if meanwhile:
        meanwhile()
    return matmul_stage(K, KT, n_f, lambda k: hidden[:, k, 0:T], T,
                        lambda e, m, ps: e.activation(y[:, m, 0:T], ps, ACT.Copy), [],
                        k_ready=lambda k: [(mixed, h + k + 1)], banks=(4, 5, 6, 7), squares=True)


class Area:

    def __init__(self, *regions):
        self.regions = [[r, 0] for r in regions]

    def get(self, *shape):
        n = int(np.prod(shape))
        for r in self.regions:
            if r[1] + n <= r[0].shape[-1]:
                ap = r[0][:, r[1]:r[1] + n]
                r[1] += n
                if len(shape) == 1:
                    return ap
                names = "abcd"[:len(shape)]
                return ap.rearrange(f"p ({' '.join(names)}) -> p {' '.join(names)}", **{x: y for x, y in zip(names, shape)})
        raise ValueError(f"no room for {shape}: {[(r[0].shape, r[1]) for r in self.regions]}")


def bc(ap, axis, n):
    ap = ap.unsqueeze(axis)
    return ap.to_broadcast([n if i == axis else s for i, s in enumerate(ap.shape)])


def gate_stage(K, u, rows2, kpe, G, deps, k_ready):
    made, out, at_act, at_dve, done = (K.counter(n) for n in ("gate_products", "gate_out", "gate_scalar", "gate_vector", "gates_ready"))
    b, o = made.reserve(3), out.reserve(1)
    sa, sv, rd = at_act.reserve(5), at_dve.reserve(3), done.reserve(1)
    first = K.next_blocks(KT, (made, b + 2))
    x, mag, ex, lg, g, beta, ea, gc, egc, ekd, gl_raw, gl, diff = (G[n] for n in ("x", "mag", "ex", "lg", "g", "beta", "ea", "gc", "egc", "ekd", "gl_raw", "gl", "diff"))
    sums = K.bank(3, 256)

    def tensor(pe):
        need(pe, deps)
        for k in range(KT):
            K.arrived(pe, first + k)
            for t in range(4):
                mm = pe.matmul(K.bank(4 + t, 32), u[:, k, t * P:t * P + P], K.block(first + k)[:, 0:32], start=(k == 0), stop=(k == KT - 1))
        mm.then_inc(made.sem, 1)
        for k in range(KT):
            mm = pe.matmul(K.psum[64:96, 0, :], K.block(first + k)[:, 64:96], u[:, k, :], start=(k == 0), stop=(k == KT - 1))
        mm.then_inc(made.sem, 1)
        pe.wait_ge(at_dve.sem, sv + 2)
        for d in range(2):
            pe.matmul(sums[:, 32 * d:32 * d + 32].rearrange("p (t h) -> p t h", t=4), K.c("upto")[:, P * d:P * d + P], g[:, :, 8 * d:8 * d + 8], start=True, stop=True)
        pe.matmul(sums[:, 64:128], K.c("halves"), g.rearrange("p t h -> p (t h)"), start=True, stop=True)
        for j in range(2):
            mm = pe.matmul(sums[:, 128 + 64 * j:192 + 64 * j], K.c("chunk")[:, P * j:P * j + P], g.rearrange("p t h -> p (t h)"), start=True, stop=True)
        mm.then_inc(made.sem, 1)

    ab = K.psum[:, 4:8, 0:32]

    def vector(dve):
        step = K.in_turn(dve, "vector")
        dve.wait_ge(made.sem, b + 1)
        dve.tensor_tensor(out=x, in0=ab[:, :, 0:16], in1=bc(rows2[:, 16:32], 1, 4), op=ALU.add).then_inc(at_dve.sem, 1)
        dve.wait_ge(at_act.sem, sa + 4)
        step(dve.scalar_tensor_tensor(out=g, in0=x, scalar=0.0, in1=lg, op0=ALU.max, op1=ALU.add))
        dve.scalar_tensor_tensor(out=g, in0=g, scalar=-1.0, in1=bc(ea, 1, 4), op0=ALU.mult, op1=ALU.mult).then_inc(at_dve.sem, 1)
        dve.wait_ge(made.sem, b + 3)
        step(dve.tensor_copy(gc.rearrange("p d t h -> p (d t h)"), sums[:, 0:64]))
        dve.tensor_tensor(out=diff, in0=sums[:, 64:128].rearrange("p (t d h) -> p d t h", t=4, d=2), in1=gc, op=ALU.subtract).then_inc(at_dve.sem, 1)
        dve.wait_ge(at_act.sem, sa + 5)
        for p in range(2):
            ins = dve.tensor_copy(gl[64 * p:64 * p + 64].rearrange("p j n h -> p (j n) h"), gl_raw[64 * p:64 * p + 64].rearrange("p j t (n h) -> p (j t n) h", h=4)[:, p::2, :])
        ins.then_inc(done.sem, 1)

    def scalar(act):
        step = K.in_turn(act, "scalar")
        act.wait_ge(made.sem, b + 2)
        act.activation(kpe[64:96, :], K.psum[64:96, 0, :], ACT.Copy).then_inc(out.sem, 1)
        act.activation(ea, rows2[:, 0:16], ACT.Exp).then_inc(at_act.sem, 1)
        act.wait_ge(at_dve.sem, sv + 1)
        act.activation(beta, ab[:, :, 16:32], ACT.Sigmoid).then_inc(at_act.sem, 1)
        step(act.activation(mag, x, ACT.Abs))
        act.activation(ex, mag, ACT.Exp, scale=-1.0).then_inc(at_act.sem, 1)
        act.wait_ge(at_act.sem, sa + 3)
        act.activation(lg, ex, ACT.Ln, bias=1.0).then_inc(at_act.sem, 1)
        act.wait_ge(made.sem, b + 3)
        act.wait_ge(at_dve.sem, sv + 3)
        act.activation(egc.rearrange("p d t h -> p (d t h)"), sums[:, 0:64], ACT.Exp)
        act.activation(ekd, diff, ACT.Exp)
        act.activation(gl_raw.rearrange("p j t h -> p (j t h)"), sums[:, 128:256], ACT.Exp).then_inc(at_act.sem, 1)

    K.add(tensor=tensor, vector=vector, scalar=scalar)
    return [(out, o + 1), (done, rd + 1), (at_act, sa + 5)]


def turn_stage(K, src, dst, deps):
    turned, out = K.counter("turned_tiles"), K.counter("turned_tiles_out")
    b, e = turned.reserve(4), out.reserve(4)

    def tensor(pe):
        need(pe, deps)
        for t in range(4):
            if t >= 2:
                pe.wait_ge(out.sem, e + t - 1)
            for m in range(4):
                mm = pe.transpose(K.bank(6 + t % 2)[:, m * P:m * P + P], src[:, m, t * P:t * P + P], K.c("ident"))
            mm.then_inc(turned.sem, 1)

    def scalar(act):
        for t in range(4):
            act.wait_ge(turned.sem, b + t + 1)
            act.activation(dst[:, t, :], K.bank(6 + t % 2), ACT.Copy).then_inc(out.sem, 1)

    K.add(tensor=tensor, scalar=scalar)
    return [(out, e + 4)]


def delta_unit(K, B, G, d, t, fill, adds, deps):
    names = ("d_rowsum", "d_erow", "d_diff", "d_decay", "d_kb", "d_kbT", "d_kbT_out", "d_raw", "d_mats", "d_mask", "d_prod", "d_prod_out", "d_pair", "d_grown", "d_uw", "d_uw_out", "d_vp", "d_new", "d_su", "d_state", "d_o", "d_o_out", "d_ug")
    sg = {n: K.counter(n) for n in names}
    cnt = {"d_mask": 12, "d_prod": 12, "d_prod_out": 10, "d_pair": 10, "d_grown": 12, "d_vp": 2, "d_new": 2, "d_su": 2, "d_state": 2}
    at = {n: sg[n].reserve(cnt.get(n, 1)) for n in names}
    A, E, C, X, Y = B["mats"]
    kb, kbe, kd, vb, kbT, QK, U, W, QD, new = (B[n] for n in ("kb", "kbe", "kd", "vb", "kbT", "QK", "U", "W", "QD", "new"))
    qT, kT, ktok, vtok, O = B["qT"], B["kT"], B["ktok"], B["vtok"], B["O"]
    states = B["states"][d]
    s0 = B["turn"][d]
    B["turn"][d] = (s0 + 2) % 3
    ts = slice(t * P, t * P + P)
    order = (0, 1) if d == 0 else (1, 0)
    upto = K.c("upto")[:, P * d:P * d + P]
    level = K.c("levels").rearrange("p (l n) -> p l n", n=P)
    hh = slice(8 * d, 8 * d + 8)
    four = lambda n: K.bank(n).rearrange("p (h n) -> p h n", n=P)
    two = lambda n: K.psum[:, n:n + 2, :].rearrange("p b (h n) -> p (b h) n", n=P)

    def hit(eng, name, k=1):
        eng.wait_ge(sg[name].sem, at[name] + k)

    def hs(m, h):
        return m[:, 4 * (h % 2) + h // 2, :]

    def tensor(pe):
        need(pe, deps)
        hit(pe, "d_ug")
        for b in range(2):
            mm = pe.matmul(K.bank(b), K.c("ones"), A[:, 4 * b:4 * b + 4, :].rearrange("p h n -> p (h n)"), start=True, stop=True)
        mm.then_inc(sg["d_rowsum"].sem, 1)
        if fill[0]:
            fill[0].turn(pe)
        if fill[1]:
            fill[1].product(pe)
        hit(pe, "d_kb")
        for i in range(4):
            mm = pe.transpose(K.bank(2)[:, i * P:i * P + P], kb[:, i * P:i * P + P], K.c("ident"))
        mm.then_inc(sg["d_kbT"].sem, 1)
        hit(pe, "d_kbT_out")
        if fill[0]:
            need(pe, fill[0].after(3))
        for h in range(HEADS):
            p, i = 64 * (h % 2), h // 2
            pe.matmul(K.bank(4 + h % 2)[:, i * P:i * P + P], kT[p:p + 64, i, ts], kbT[p:p + 64, i, :], start=True, stop=True)
            mm = pe.matmul(K.bank(6 + h % 2)[:, i * P:i * P + P], kT[p:p + 64, i, ts], qT[p:p + 64, i, ts], start=True, stop=True)
        mm.then_inc(sg["d_raw"].sem, 1)
        if fill[1]:
            fill[1].turn(pe)
        if fill[2]:
            fill[2].product(pe)
        for lv in range(6):
            for gr in range(2):
                hit(pe, "d_mask", 2 * lv + gr + 1)
                if lv:
                    hit(pe, "d_grown", 2 * lv - 1 + gr)
                for n in range(4):
                    m = 4 * gr + n
                    mm = pe.matmul(K.bank(gr)[:, n * P:n * P + P], E[:, m, :], X[:, m, :] if lv else K.c("ident"), start=True, stop=True)
                mm.then_inc(sg["d_prod"].sem, 1)
            if lv == 1:
                for c, i in ((fill[1], 3), (fill[2], 1)):
                    if c:
                        need(pe, c.after(i))
            for gr in range(2 if lv else 0):
                hit(pe, "d_prod_out", 2 * lv - 1 + gr)
                for n in range(4):
                    m = 4 * gr + n
                    if lv < 5:
                        pe.matmul(K.bank(2 + gr)[:, n * P:n * P + P], Y[:, m, :], A[:, m, :], start=True, stop=True)
                    mm = pe.matmul(K.bank(4 + gr)[:, n * P:n * P + P], A[:, m, :], Y[:, m, :], start=True, stop=True)
                mm.then_inc(sg["d_pair"].sem, 1)
        hit(pe, "d_grown", 12)
        for h in range(HEADS):
            p, i = 64 * (h % 2), h // 2
            pe.matmul(K.bank(0)[:, 64 * h:64 * h + 64], hs(Y, h), vb[:, 64 * h:64 * h + 64], start=True, stop=True)
            mm = pe.matmul(K.psum[p:p + 64, 1, i * P:i * P + P], kbe[:, 64 * h:64 * h + 64], hs(Y, h), start=True, stop=True)
        mm.then_inc(sg["d_uw"].sem, 1)
        if fill[2]:
            fill[2].turn(pe)
        if fill[3]:
            fill[3].product(pe)
        hit(pe, "d_uw_out")
        for n, j in enumerate(order):
            st = states[(s0 + n) % 3]
            c = slice(64 * j, 64 * j + 64)
            if n:
                hit(pe, "d_state", 1)
            for h in range(HEADS):
                p, i = 64 * (h % 2), h // 2
                mm = pe.matmul(K.psum[c, 2 + h % 2, 64 * i:64 * i + 64], W[p:p + 64, i, c], st[p:p + 64, i, :], start=True, stop=True)
            mm.then_inc(sg["d_vp"].sem, 1)
            hit(pe, "d_new", n + 1)
            for h in range(HEADS):
                p, i = 64 * (h % 2), h // 2
                mm = pe.matmul(K.psum[p:p + 64, 4 + n, 64 * i:64 * i + 64], kd[c, 64 * h:64 * h + 64], new[c, 64 * h:64 * h + 64], start=True, stop=True)
            mm.then_inc(sg["d_su"].sem, 1)
        if fill[2]:
            need(pe, fill[2].after(3))
        for h in range(HEADS):
            p, i = 64 * (h % 2), h // 2
            o = K.psum[p:p + 64, 6, i * P:i * P + P]
            pe.matmul(o, new[:, 64 * h:64 * h + 64], hs(QK, h), start=True, stop=False)
            for n, j in enumerate(order):
                mm = pe.matmul(o[:, 64 * j:64 * j + 64], states[(s0 + n) % 3][p:p + 64, i, :], QD[p:p + 64, i, 64 * j:64 * j + 64], start=False, stop=(n == 1))
        mm.then_inc(sg["d_o"].sem, 1)

    def scalar(act):
        need(act, deps)
        hit(act, "d_diff")
        act.activation(C, two(0), ACT.Exp).then_inc(sg["d_erow"].sem, 1)
        act.activation(E, E, ACT.Exp).then_inc(sg["d_decay"].sem, 1)
        if fill[1]:
            fill[1].keep(act)
        hit(act, "d_kbT")
        act.activation(kbT.rearrange("p i n -> p (i n)"), K.bank(2), ACT.Copy).then_inc(sg["d_kbT_out"].sem, 1)
        if fill[2]:
            fill[2].keep(act)
        for lv in range(1, 6):
            for gr in range(2):
                hit(act, "d_prod", 2 * lv + gr + 1)
                act.activation(A[:, 4 * gr:4 * gr + 4, :], four(gr), ACT.Copy).then_inc(sg["d_prod_out"].sem, 1)
        hit(act, "d_uw")
        act.activation(U, K.bank(0), ACT.Copy)
        act.activation(W.rearrange("p i n -> p (i n)"), K.bank(1), ACT.Copy).then_inc(sg["d_uw_out"].sem, 1)
        if fill[3]:
            fill[3].keep(act)

    def vector(dve):
        step = K.in_turn(dve, "vector")
        need(dve, deps)
        nat = lambda m: m.rearrange("p (i q n) -> p q i n", i=4, q=2)
        def coef(m):
            return bc(m.rearrange("p (q i) -> p q i", q=2), 3, 64)
        dve.tensor_tensor(out=A, in0=bc(upto, 1, 8), in1=bc(G["g"][:, t, hh], 2, P), op=ALU.mult).then_inc(sg["d_ug"].sem, 1)
        dve.tensor_tensor(out=nat(kb), in0=nat(ktok[:, t, :]), in1=coef(G["beta"][:, t, hh]), op=ALU.mult).then_inc(sg["d_kb"].sem, 1)
        dve.tensor_tensor(out=nat(vb), in0=nat(vtok[:, t, :]), in1=coef(G["beta"][:, t, hh]), op=ALU.mult)
        dve.tensor_tensor(out=nat(kd), in0=nat(ktok[:, t, :]), in1=coef(G["ekd"][:, d, t, :]), op=ALU.mult)
        hit(dve, "d_kb")
        dve.tensor_tensor(out=nat(kbe), in0=nat(kb), in1=coef(G["egc"][:, d, t, :]), op=ALU.mult)
        hit(dve, "d_rowsum")
        rows = two(0)
        for n in range(8):
            ins = dve.tensor_scalar(E[:, n, :], rows[:, n, :], G["gc"][:, d, t, n:n + 1], 0.0, ALU.subtract, ALU.min)
        ins.then_inc(sg["d_diff"].sem, 1)
        if fill[0]:
            fill[0].add(dve)
        hit(dve, "d_erow")
        for p in range(2):
            q = slice(64 * p, 64 * p + 64)
            ins = dve.tensor_tensor(out=QD[q], in0=qT[q, :, ts], in1=C[q, 4 * p:4 * p + 4, :], op=ALU.mult)
        step(ins)
        hit(dve, "d_decay")
        step(dve.tensor_tensor(out=E, in0=E, in1=bc(upto, 1, 8), op=ALU.mult))
        hit(dve, "d_raw")
        dve.tensor_tensor(out=QK, in0=two(6), in1=E, op=ALU.mult)
        step(dve.tensor_tensor(out=C, in0=two(4), in1=E, op=ALU.mult))
        def mask(lv, gr):
            g = slice(4 * gr, 4 * gr + 4)
            dve.tensor_tensor(out=E[:, g, :], in0=C[:, g, :], in1=bc(level[:, 6 * d + lv, :], 1, 4), op=ALU.mult).then_inc(sg["d_mask"].sem, 1)

        for gr in range(2):
            mask(0, gr)
        if fill[1]:
            fill[1].add(dve)
        for lv in range(6):
            for gr in range(2):
                g = slice(4 * gr, 4 * gr + 4)
                if lv == 0:
                    hit(dve, "d_mask", gr + 1)
                    dve.scalar_tensor_tensor(out=Y[:, g, :], in0=E[:, g, :], scalar=-1.0, in1=bc(K.c("ident"), 1, 4), op0=ALU.mult, op1=ALU.add)
                    hit(dve, "d_prod", gr + 1)
                    dve.scalar_tensor_tensor(out=X[:, g, :], in0=four(gr), scalar=-1.0, in1=bc(K.c("ident"), 1, 4), op0=ALU.mult, op1=ALU.add).then_inc(sg["d_grown"].sem, 1)
                    continue
                hit(dve, "d_pair", 2 * lv - 1 + gr)
                if lv < 5:
                    dve.tensor_tensor(out=X[:, g, :], in0=X[:, g, :], in1=four(2 + gr), op=ALU.subtract)
                dve.tensor_tensor(out=Y[:, g, :], in0=Y[:, g, :], in1=four(4 + gr), op=ALU.subtract).then_inc(sg["d_grown"].sem, 1)
            for gr in range(2 if lv < 5 else 0):
                hit(dve, "d_prod", 2 * lv + gr + 1)
                hit(dve, "d_grown", 2 * lv + gr + 1)
                mask(lv + 1, gr)
        if fill[2]:
            fill[2].add(dve)
        hit(dve, "d_uw_out")
        for n, j in enumerate(order):
            c = slice(64 * j, 64 * j + 64)
            st, nx = states[(s0 + n) % 3], states[(s0 + n + 1) % 3]
            hit(dve, "d_vp", n + 1)
            dve.tensor_tensor(out=nat(new[c]), in0=nat(U[c]), in1=K.psum[c, 2:4, 0:256].rearrange("p q (i n) -> p q i n", i=4), op=ALU.subtract).then_inc(sg["d_new"].sem, 1)
            step(dve.tensor_tensor(out=nx, in0=st, in1=bc(G["gl"][:, j, 2 * t + d, :], 2, 64), op=ALU.mult))
            hit(dve, "d_su", n + 1)
            dve.tensor_tensor(out=nx, in0=nx, in1=K.bank(4 + n, 256).rearrange("p (i n) -> p i n", i=4), op=ALU.add).then_inc(sg["d_state"].sem, 1)
            hit(dve, "d_state", n + 1)
        hit(dve, "d_o")
        o = K.bank(6).rearrange("p (i n) -> p i n", i=4)
        if adds:
            dve.tensor_tensor(out=O[:, :, ts], in0=O[:, :, ts], in1=o, op=ALU.add).then_inc(sg["d_o_out"].sem, 1)
        else:
            dve.tensor_copy(O[:, :, ts], o).then_inc(sg["d_o_out"].sem, 1)

    K.add(tensor=tensor, scalar=scalar, vector=vector)
    return [(sg["d_o_out"], at["d_o_out"] + 1), (sg["d_uw_out"], at["d_uw_out"] + 1)]


def even_mixer(K, R, u, deps, k_ready, mod_pieces):
    T = T2
    area = Area(R.arena)
    qkvT, gate = area.get(12, T), area.get(4, T)
    qd, kvd, kpe = area.get(2, T), area.get(1, T), area.get(T)
    conv_area = Area(R.arena[:, 10240:], R.y)
    pads = [conv_area.get(2, S + 4) for _ in range(2)]
    conv = [conv_area.get(2, S) for _ in range(2)]
    G = R.gate
    padded, clear, convolved, silued = (K.counter(n) for n in ("padded", "cleared", "convolved", "silued"))
    taps = K.v("gdn_conv").rearrange("p (m j) -> p m j", j=5)
    made = K.counter("products")
    b, pb, cb, cv, si = made.reserve(16), padded.reserve(12), clear.reserve(1), convolved.reserve(12), silued.reserve(12)
    go = K.counter("gate_tiles")
    gb = go.reserve(4)
    first = [K.next_blocks(KT, (made, b + m + 1)) for m in range(16)]

    def tensor(pe):
        need(pe, deps)
        for m in range(16):
            if m >= 4:
                pe.wait_ge(padded.sem, pb + min(m - 3, 12))
            for k in range(KT):
                if m == 0:
                    need(pe, k_ready(k))
                K.arrived(pe, first[m] + k)
                mm = pe.matmul(K.bank(m % 4), K.block(first[m] + k), u[:, k, :], start=(k == 0), stop=(k == KT - 1))
            mm.then_inc(made.sem, 1)

    def gpsimd(pool):
        for x in pads:
            ins = pool.memset(x, 0.0)
        ins.then_inc(clear.sem, 1)

    def scalar(act):
        act.wait_ge(clear.sem, cb + 1)
        for m in range(17):
            if m < 12:
                act.wait_ge(made.sem, b + m + 1)
                if m >= 2:
                    act.wait_ge(convolved.sem, cv + m - 1)
                act.activation(pads[m % 2][:, :, 2:2 + S], K.bank(m % 4).rearrange("p (s n) -> p s n", s=2), ACT.Copy).then_inc(padded.sem, 1)
            if 1 <= m <= 12:
                act.wait_ge(convolved.sem, cv + m)
                act.activation(qkvT[:, m - 1, :].rearrange("p (s n) -> p s n", s=2), conv[(m - 1) % 2], ACT.Silu).then_inc(silued.sem, 1)
            if 12 <= m < 16:
                act.wait_ge(made.sem, b + m + 1)
                act.activation(gate[:, m - 12, :], K.bank(m % 4), ACT.Silu).then_inc(go.sem, 1)

    def vector(dve):
        step = K.in_turn(dve, "vector")
        for m in range(12):
            dve.wait_ge(padded.sem, pb + m + 1)
            if m >= 2:
                dve.wait_ge(silued.sem, si + m - 1)
            x, o = pads[m % 2], conv[m % 2]
            step(dve.tensor_scalar(o, x[:, :, 0:S], taps[:, m, 0:1], None, ALU.mult))
            for j in range(1, 5):
                ins = dve.scalar_tensor_tensor(out=o, in0=x[:, :, j:j + S], scalar=taps[:, m, j:j + 1], in1=o, op0=ALU.mult, op1=ALU.add)
                if j < 4:
                    step(ins)
            ins.then_inc(convolved.sem, 1)

    K.add(tensor=tensor, scalar=scalar, vector=vector, gpsimd=gpsimd)
    ready_qkv, ready_gate = [(silued, si + 12)], [(go, gb + 4)]

    ready_g = gate_stage(K, u, R.rows, kpe, G, ready_gate, lambda k: [])
    lora = matmul_stage(K, 3, KT, lambda k: u[:, k, :], T,
                        lambda e, m, ps: e.activation((qd[:, m, :] if m < 2 else kvd[:, 0, :]), ps, ACT.Copy), ready_g)

    def unit(dve, g, r, emit):
        x = qkvT[:, g, :]
        if g < 4:
            emit(dve.scalar_tensor_tensor(out=x, in0=x, scalar=CHUNK ** -0.5, in1=r, op0=ALU.mult, op1=ALU.mult))
        else:
            emit(dve.tensor_tensor(out=x, in0=x, in1=r, op=ALU.mult))
    _, _, unit_ready = scale_stage(K, [[qkvT[:, g, :]] for g in range(8)], T, K.c("halves"), 1.0, unit, ready_qkv + lora)

    ga = Area(R.u, R.y, R.arena[:, 10240:], R.m[:, 2048:])
    B = {"mats": [ga.get(8, P) for _ in range(5)], "ktok": ga.get(4, 512), "vtok": ga.get(4, 512)}
    for n in ("kb", "kbe", "kd", "vb", "U", "new"):
        B[n] = ga.get(512)
    B["kbT"], B["W"], B["QD"] = ga.get(4, P), ga.get(4, P), ga.get(4, P)
    B["QK"] = ga.get(8, P)
    B["qT"], B["kT"] = qkvT[:, 0:4, :], qkvT[:, 4:8, :]
    B["O"] = R.m[:, 0:2048].rearrange("p (i n) -> p i n", i=4)
    st = Area(qkvT[:, 8:12, :].rearrange("p i n -> p (i n)"))
    B["states"] = [[st.get(4, 64) for _ in range(3)] for _ in range(2)]
    B["turn"] = [0, 0]
    r1 = turn_stage(K, qkvT[:, 4:8, :], B["ktok"], unit_ready)
    r2 = turn_stage(K, qkvT[:, 8:12, :], B["vtok"], r1)
    zero = K.counter("states_cleared")
    z = zero.reserve(1)

    def clear_states(pool):
        need(pool, r2)
        for d in range(2):
            ins = pool.memset(B["states"][d][0], 0.0)
        ins.then_inc(zero.sem, 1)

    K.add(gpsimd=clear_states)
    ready = r1 + r2 + [(zero, z + 1)] + ready_g
    seen = set()
    carried = None
    for d, t in ((0, 0), (1, 1), (0, 1), (1, 0), (0, 2), (1, 3), (0, 3), (1, 2)):
        own = [mod_pieces.pop(0)(*banks) if mod_pieces else None for banks in ((3, 3), (2, 6), (7, 7))]
        ready = delta_unit(K, B, G, d, t, [carried] + own, t in seen, ready)
        carried = own[2]
        seen.add(t)
    assert not mod_pieces and carried is None

    O = B["O"]

    def gated(dve, g, r, emit):
        step = K.in_turn(dve, "vector")
        step(dve.scalar_tensor_tensor(out=O[:, g, :], in0=O[:, g, :], scalar=K.v("gdn_out_norm"), in1=r, op0=ALU.mult, op1=ALU.mult))
        emit(dve.tensor_tensor(out=O[:, g, :], in0=O[:, g, :], in1=gate[:, g, :], op=ALU.mult))
    _, _, gdn_ready = scale_stage(K, [[O[:, g, :]] for g in range(4)], T, K.c("halves"), 1.0 / 64, gated, ready)

    def normed(x, gain):
        def apply(dve, g, r, emit):
            for k, ap in enumerate(x):
                ins = dve.scalar_tensor_tensor(out=ap, in0=ap, scalar=gain[:, k:k + 1], in1=r, op0=ALU.mult, op1=ALU.mult)
            emit(ins)
        return apply
    _, _, rq = scale_stage(K, [[qd[:, 0, :], qd[:, 1, :]]], T, K.c("ones"), 1.0 / 256, normed([qd[:, 0, :], qd[:, 1, :]], K.v("mla_q_norm")), gdn_ready)
    _, _, rk = scale_stage(K, [[kvd[:, 0, :]]], T, K.c("ones"), 1.0 / 128, normed([kvd[:, 0, :]], K.v("mla_kv_norm")), rq)
    ma = Area(R.u, R.y, R.arena)
    q, k = ma.get(8, T), ma.get(8, T)
    ma = Area(R.arena[:, 10240:], R.arena[:, 0:8192])
    values = ma.get(4, 8, P)
    buf = attention_buffers(K, ma)
    tmp = ma.get(2, T)
    filled, fb = K.counter("ones_filled"), None
    fb = filled.reserve(1)
    K.add(gpsimd=lambda pool: (need(pool, rk), pool.memset(values, 1.0).then_inc(filled.sem, 1)))
    mq = matmul_stage(K, HEADS, 2, lambda kk: qd[:, kk, :], T, lambda e, m, ps: e.activation(q[0:96, m, :], ps, ACT.Copy), rk + rq, rows=lambda m: (0, 96))

    def nope(e, m, ps):
        e.activation(k[0:64, 2 * m, :], ps[0:64, :], ACT.Copy)
        return e.activation(k[0:64, 2 * m + 1, :], ps[64:128, :], ACT.Copy)
    mk = matmul_stage(K, 4, 1, lambda kk: kvd[:, 0, :], T, nope, mq)

    def value(e, t, ps):
        v = ps.rearrange("p (i q n) -> p i q n", i=4, q=2)
        o = values[:, t].rearrange("p (i q) n -> p i q n", q=2)
        e.activation(o[:, :, 0, 0:64], v[:, :, 0, :], ACT.Copy)
        return e.activation(o[:, :, 1, 64:128], v[:, :, 1, :], ACT.Copy)
    mv = token_stage(K, 1, 512, lambda kk, t: kvd[:, 0, t * P:t * P + P], 4, value, mk + [(filled, fb + 1)])
    lat = slice(S, T2)
    items = [(q[0:96, h, lat], 0, 96, K.c("mla_cos")[0:96], K.c("mla_sin")[0:96], q[0:96, h, lat]) for h in range(HEADS)]
    items.append((kpe[64:96, lat], 64, 96, K.c("mla_cos")[64:96], K.c("mla_sin")[64:96], kpe[64:96, lat]))
    rr = rope_stage(K, items, K.c("rot_mla"), S, mv, tmp)
    spread, sb = K.counter("rotary_key_spread"), None
    sb = spread.reserve(1)
    K.add(vector=lambda dve: (need(dve, rr), dve.tensor_copy(k[64:96], bc(kpe[64:96, :], 1, 8)).then_inc(spread.sem, 1)))
    ready = rr + [(spread, sb + 1)] + mv + mk
    for c0, length in ((S, T2), (0, S)):
        ready = attention_stage(K, HEADS, length, 2, 96 ** -0.5,
                                lambda h, t, c0=c0: q[0:96, h, c0 + t * P:c0 + t * P + P], lambda h, n=length: k[0:96, h, 0:n],
                                lambda h, kt: values[:, kt, h, :], None,
                                lambda h, c0=c0: R.mix[64 * (h % 2):64 * (h % 2) + 64, 4 + h // 2, c0:c0 + S], ready, buf)
    return ready + gdn_ready


def attention_buffers(K, area):
    return area.get(2, 512), area.get(2, 4, 2 * P), K.small, area.get(2 * P)


def odd_mixer(K, R, u, deps, k_ready, table_ready):
    area = Area(R.arena, R.y)
    nq, gq, nk, gk = area.get(4, S), area.get(4, S), area.get(4, T2), area.get(1, T2)
    nv, gv = area.get(4, 8, P), area.get(4, 2, P)
    buf = attention_buffers(K, area)
    tmp = area.get(2, T2)
    lat = slice(S, T2)
    filled = K.counter("ones_filled")
    fb = filled.reserve(1)

    def fill(pool):
        need(pool, deps)
        pool.memset(nv, 1.0)
        pool.memset(gv, 1.0).then_inc(filled.sem, 1)
    K.add(gpsimd=fill)
    r = matmul_stage(K, 8, KT, lambda k: u[:, k, lat], S,
                     lambda e, m, ps: e.activation(nq[:, m, :] if m < 4 else gq[:, m - 4, :], ps, ACT.Copy), deps, k_ready=k_ready)
    r = matmul_stage(K, 5, KT, lambda k: u[:, k, :], T2,
                     lambda e, m, ps: e.activation(nk[:, m, :] if m < 4 else gk[:, 0, :], ps, ACT.Copy), r)

    def value(e, t, ps):
        v = ps.rearrange("p (i q n) -> p i q n", i=4, q=2)
        o = nv[:, t].rearrange("p (i q) n -> p i q n", q=2)
        e.activation(o[:, :, 0, 0:64], v[:, :, 0, :], ACT.Copy)
        return e.activation(o[:, :, 1, 64:128], v[:, :, 1, :], ACT.Copy)

    def group_value(e, t, ps):
        e.activation(gv[:, t, 0, 0:64], ps[:, 0:64], ACT.Copy)
        return e.activation(gv[:, t, 1, 64:128], ps[:, 64:128], ACT.Copy)
    tokens = lambda k, t: u[:, k, t * P:t * P + P]
    r = token_stage(K, KT, 512, tokens, 4, value, r + [(filled, fb + 1)])
    r = token_stage(K, KT, P, tokens, 4, group_value, r)

    def head_norm(x, gain):
        def apply(dve, g, rs, emit):
            emit(dve.scalar_tensor_tensor(out=x(g), in0=x(g), scalar=K.v(gain), in1=rs, op0=ALU.mult, op1=ALU.mult))
        return apply
    _, _, r = scale_stage(K, [[gq[:, g, :]] for g in range(4)], S, K.c("halves"), 1.0 / 64, head_norm(lambda g: gq[:, g, :], "gqa_q_norm"), r)
    _, _, r = scale_stage(K, [[gk[:, 0, :]]], T2, K.c("halves"), 1.0 / 64, head_norm(lambda g: gk[:, 0, :], "gqa_k_norm"), r)
    items = [(x, 0, P, K.c("gqa_cos"), K.c("gqa_sin"), x) for x in [gq[:, g, :] for g in range(4)] + [gk[:, 0, lat]]]
    r = rope_stage(K, items, K.c("rot_gqa"), S, r, tmp)
    table = R.table
    r = attention_stage(K, HEADS, T2, 2, 64 ** -0.5,
                        lambda h, t: nq[64 * (h % 2):64 * (h % 2) + 64, h // 2, t * P:t * P + P],
                        lambda h: nk[64 * (h % 2):64 * (h % 2) + 64, h // 2, :], lambda h, kt: nv[:, kt, h, :],
                        lambda h, t: table[:, h, t, :], lambda h: R.mixed[64 * (h % 2):64 * (h % 2) + 64, h // 2, :], r + table_ready, buf, "mirror")
    return attention_stage(K, HEADS, T2, 2, 64 ** -0.5,
                           lambda h, t: gq[64 * (h % 2):64 * (h % 2) + 64, h // 2, t * P:t * P + P],
                           lambda h: gk[64 * (h % 2):64 * (h % 2) + 64, 0, :], lambda h, kt: gv[:, kt, h % 2, :],
                           None, lambda h: R.mixed[64 * (h % 2):64 * (h % 2) + 64, 4 + h // 2, :], r, buf)


def bias_load(K, R, rpb, deps):
    loaded = K.counter("bias_loaded")
    lb = loaded.reserve(16 * 4 * HEADS)

    def gpsimd(pool):
        need(pool, deps)
        for r in range(4):
            for h in range(HEADS):
                src = bass.AP(rpb.tensor, rpb.offset + (h * 15 + 7 - r) * 31 + 15 - 63, [[1, 64], [31, 4], [1, 64]])
                pool.dma_start(R.table[64 * (r % 2):64 * (r % 2) + 64, h, r // 2, :].rearrange("p (a b) -> p a b", a=4), src).then_inc(loaded.sem, 16)

    K.add(gpsimd=gpsimd)
    return [(loaded, lb + 16 * 4 * HEADS)]


def bias_window(K, R, deps):
    done = K.counter("bias_ready")
    db = done.reserve(1)

    def vector(dve):
        need(dve, deps)
        step = K.in_turn(dve, "vector")
        flat = R.table.rearrange("p h t (r c) -> p (h t r) c", c=64)
        step(dve.scalar_tensor_tensor(out=flat, in0=flat, scalar=8.0, in1=bc(K.c("window"), 1, 64), op0=ALU.mult, op1=ALU.mult))
        dve.tensor_tensor(out=flat, in0=flat, in1=bc(K.c("outside"), 1, 64), op=ALU.add).then_inc(done.sem, 1)

    K.add(vector=vector)
    return [(done, db + 1)]


def position_tables(K, R, deps):
    a, b = K.counter("angles"), K.counter("sines")
    ab, sb = a.reserve(1), b.reserve(1)
    ang, turns, quarter = R.angle, R.turns, R.quarter
    two_pi = 2 * np.pi
    c1 = 6.28125
    c2 = float(np.float32(np.round((two_pi - c1) * 2 ** 22) / 2 ** 22))
    c3 = float(np.float32(two_pi - c1 - c2))

    def vector(dve):
        need(dve, deps)
        step = K.in_turn(dve, "vector")
        step(dve.tensor_copy(ang, R.positions))
        step(dve.tensor_scalar(ang, ang, K.c("dsa_freq"), None, ALU.mult))
        step(dve.tensor_scalar(turns, ang, 1.0 / two_pi, 12582912.0, ALU.mult, ALU.add))
        step(dve.tensor_scalar(turns, turns, 12582912.0, None, ALU.subtract))
        for part in (c1, c2, c3):
            step(dve.scalar_tensor_tensor(out=ang, in0=turns, scalar=-part, in1=ang, op0=ALU.mult, op1=ALU.add))
        dve.tensor_scalar(ang, ang, 3.1415925, -3.1415925, ALU.min, ALU.max).then_inc(a.sem, 1)

    def scalar(act):
        act.wait_ge(a.sem, ab + 1)
        K.in_turn(act, "scalar")(act.activation(quarter, ang, ACT.Abs))
        act.activation(R.dsa_sin, ang, ACT.Sin)
        act.activation(R.dsa_cos, quarter, ACT.Sin, bias=K.c("half_pi"), scale=-1.0).then_inc(b.sem, 1)

    K.add(vector=vector, scalar=scalar)
    return [(b, sb + 1)]


def sparse_mixer(K, R, layer, u, deps, k_ready):
    area = Area(R.arena, R.y)
    q, kk, qi, ki = area.get(4, S), area.get(1, S), area.get(8, S), area.get(1, S)
    ga, gs = area.get(2, S), area.get(2, S)
    cpad = area.get(2, CONV - 1 + S)
    ppad = area.get(2, 16 + S)
    values, wi = area.get(2, 2, P), area.get(2, 16)
    buf = attention_buffers(K, area)
    tmp = area.get(2, S)
    mask = area.get(2, S)
    relu = area.get(2, S)
    work, top = area.get(S), area.get(8)
    acc, xc = area.get(2, S), area.get(2, S)
    sums = [area.get(2, 16 + S) for _ in range(4)]
    z = area.get(2, S)
    cleared = K.counter("pads_cleared")
    cb = cleared.reserve(1)

    def clear(pool):
        need(pool, deps)
        pool.memset(cpad[:, :, 0:CONV - 1], 0.0)
        pool.memset(ppad[:, :, 0:16], 0.0)
        for x in sums:
            pool.memset(x[:, :, 0:16], 0.0)
        pool.memset(values, 1.0).then_inc(cleared.sem, 1)
    K.add(gpsimd=clear)

    def take(e, m, ps):
        if m < 2:
            return e.activation(ga[:, m, :], ps, ACT.Copy)
        if m < 4:
            return e.activation(gs[:, m - 2, :], ps, ACT.Sigmoid)
        if m < 6:
            return e.activation(ppad[:, m - 4, 16:], ps, ACT.Copy)
        m -= 6
        o = q[:, m, :] if m < 4 else kk[:, 0, :] if m < 5 else qi[:, m - 5, :] if m < 13 else ki[:, 0, :]
        return e.activation(o, ps, ACT.Copy)
    out = K.counter("taken_out_by_scalar")
    r_conv = [(out, out.n + 6)]
    r = matmul_stage(K, 20, KT, lambda k: u[:, k, 0:S], S, take, deps + [(cleared, cb + 1)], k_ready=k_ready)
    conv, cd = K.counter("conv_steps"), None
    cd = conv.reserve(2)
    dw = K.v("conv_dw").rearrange("p (l m j) -> p l m j", l=2, m=2)

    def col(name, m, n=2):
        return K.v(name)[:, layer * n + m:layer * n + m + 1]

    def convolve(dve):
        need(dve, r_conv)
        step = K.in_turn(dve, "vector")
        step(dve.tensor_tensor(out=cpad[:, :, CONV - 1:], in0=ga, in1=gs, op=ALU.mult))
        for m in range(2):
            ins = dve.tensor_scalar(acc[:, m, :], cpad[:, m, 0:S], dw[:, layer, m, 0:1], col("conv_b", m), ALU.mult, ALU.add)
        step(ins)
        for j in range(1, CONV):
            for m in range(2):
                ins = dve.scalar_tensor_tensor(out=acc[:, m, :], in0=cpad[:, m, j:j + S], scalar=dw[:, layer, m, j:j + 1], in1=acc[:, m, :], op0=ALU.mult, op1=ALU.add)
            if j < CONV - 1:
                step(ins)
        ins.then_inc(conv.sem, 1)
        prev = ppad
        for n, s in enumerate(sums):
            w = 1 << n
            lo = 2 * w - 1
            step(dve.tensor_tensor(out=s[:, :, lo:], in0=prev[:, :, lo:], in1=prev[:, :, lo - w:16 + S - w], op=ALU.add))
            prev = s
        count = K.c("pool_count").rearrange("p (m n) -> p m n", m=2)
        for n, s in enumerate(sums):
            rows, m = slice(64 * (n % 2), 64 * (n % 2) + 64), n // 2
            ins = dve.tensor_tensor(out=z[rows, m, :], in0=s[rows, m, 16:], in1=count[rows, m, :], op=ALU.mult)
        step(ins)
        dve.tensor_tensor(out=z, in0=z, in1=ppad[:, :, 16:], op=ALU.subtract).then_inc(conv.sem, 1)
    K.add(vector=convolve)

    mean, centred = K.counter("channel_means"), K.counter("centred")
    mb, xb = mean.reserve(1), centred.reserve(1)

    def mean_product(pe):
        pe.wait_ge(conv.sem, cd + 1)
        for m in range(2):
            mm = pe.matmul(K.bank(6, S), K.c("ones"), acc[:, m, :], start=(m == 0), stop=(m == 1))
        mm.then_inc(mean.sem, 1)

    def centre(dve):
        dve.wait_ge(mean.sem, mb + 1)
        for m in range(2):
            ins = dve.scalar_tensor_tensor(out=xc[:, m, :], in0=K.bank(6, S), scalar=-1.0 / 256, in1=acc[:, m, :], op0=ALU.mult, op1=ALU.add)
        ins.then_inc(centred.sem, 1)
    K.add(tensor=mean_product, vector=centre)
    tokens = lambda k, t: u[:, k, t * P:t * P + P]

    def value(e, t, ps):
        e.activation(values[:, t, 0, 0:64], ps[:, 0:64], ACT.Copy)
        return e.activation(values[:, t, 1, 64:128], ps[:, 64:128], ACT.Copy)
    r = token_stage(K, KT, P, tokens, 2, value, r)
    r = token_stage(K, KT, 16, tokens, 2, lambda e, t, ps: e.activation(wi[:, t, :], ps, ACT.Copy, scale=1.0 / 32), r)


    def scaled(dve, g, rs, emit):
        for m in range(2):
            ins = dve.tensor_tensor(out=xc[:, m, :], in0=xc[:, m, :], in1=rs, op=ALU.mult)
        emit(ins)
    _, _, rc = scale_stage(K, [[xc[:, 0, :], xc[:, 1, :]]], S, K.c("ones"), 1.0 / 256, scaled, [(centred, xb + 1)], eps="ln_eps")
    act_done = K.counter("conv_activated")
    ad = act_done.reserve(1)

    def activate(act, after=rc):
        need(act, after)
        for m in range(2):
            ins = act.activation(xc[:, m, :], xc[:, m, :], ACT.Silu, bias=col("conv_ln_b", m), scale=col("conv_ln_g", m))
        ins.then_inc(act_done.sem, 1)
    K.add(scalar=activate)
    mix = R.mix2
    items = [(x, 0, P, R.dsa_cos, R.dsa_sin, x) for x in [q[:, i, :] for i in range(4)] + [kk[:, 0, :]] + [qi[:, i, :] for i in range(8)] + [ki[:, 0, :]]]
    rr = rope_stage(K, items, K.c("rot_dsa"), S, r + rc + R.positions_ready, tmp)

    dots, relued, added, masked = (K.counter(n) for n in ("index_dots", "index_relu", "index_added", "index_masked"))
    db, rb, ab, kb = dots.reserve(32), relued.reserve(32), added.reserve(32), masked.reserve(1)
    causal = K.c("causal").rearrange("p (t n) -> p t n", t=2)

    def dot_products(pe):
        need(pe, rr)
        for i in range(32):
            t, h = divmod(i, 16)
            p = 64 * (h % 2)
            if i >= 2:
                pe.wait_ge(relued.sem, rb + i - 1)
            pe.matmul(K.bank(i % 2, S), qi[p:p + 64, h // 2, t * P:t * P + P], ki[p:p + 64, 0, :], start=True, stop=True).then_inc(dots.sem, 1)

    def relus(act):
        for i in range(32):
            act.wait_ge(dots.sem, db + i + 1)
            if i >= 2:
                act.wait_ge(added.sem, ab + i - 1)
            act.activation(relu[:, i % 2, :], K.bank(i % 2, S), ACT.Relu).then_inc(relued.sem, 1)

    def select(dve):
        need(dve, rr)
        step = K.in_turn(dve, "vector")
        for t in range(2):
            for h in range(16):
                i = 16 * t + h
                dve.wait_ge(relued.sem, rb + i + 1)
                if h:
                    dve.wait_ge(added.sem, ab + i)
                    ins = dve.scalar_tensor_tensor(out=work, in0=relu[:, i % 2, :], scalar=wi[:, t, h:h + 1], in1=work, op0=ALU.mult, op1=ALU.add)
                else:
                    ins = dve.tensor_scalar(work, relu[:, i % 2, :], wi[:, t, h:h + 1], None, ALU.mult)
                ins.then_inc(added.sem, 1)
            dve.wait_ge(added.sem, ab + 16 * t + 16)
            step(dve.tensor_tensor(out=work, in0=work, in1=causal[:, t, :], op=ALU.add))
            for _ in range(TOPK // 8):
                step(dve.max(top, work))
                step(dve.match_replace(work, top, work, TAKEN))
            step(dve.tensor_scalar(mask[:, t, :], work, TAKEN / 2, NEG, ALU.is_gt, ALU.mult))
            step(dve.tensor_tensor(out=mask[:, t, :], in0=mask[:, t, :], in1=causal[:, t, :], op=ALU.add)) if t == 0 else \
                dve.tensor_tensor(out=mask[:, t, :], in0=mask[:, t, :], in1=causal[:, t, :], op=ALU.add).then_inc(masked.sem, 1)
    K.add(tensor=dot_products, scalar=relus, vector=select)
    rc = matmul_stage(K, 2, 2, lambda k: xc[:, k, :], S, lambda e, m, ps: e.activation(mix[:, 4 + m, :], ps, ACT.Copy), [(act_done, ad + 1), (relued, rb + 32)] + rc)
    for g in range(2):
        rc = matmul_stage(K, 1, 1, lambda k, g=g: z[:, g, :], S, lambda e, m, ps, g=g: e.activation(mix[:, 6 + g, :], ps, ACT.Copy, scale=col("pool_scale", g)), rc + [(conv, cd + 2)])
    ra = attention_stage(K, HEADS, S, 2, 64 ** -0.5,
                         lambda h, t: q[64 * (h % 2):64 * (h % 2) + 64, h // 2, t * P:t * P + P],
                         lambda h: kk[64 * (h % 2):64 * (h % 2) + 64, 0, :], lambda h, kt: values[:, kt, h % 2, :],
                         lambda h, t: mask[:, t, :], lambda h: mix[64 * (h % 2):64 * (h % 2) + 64, h // 2, :], [(masked, kb + 1)] + rr + rc, buf)
    return ra + rc


class Regions:
    pass


def program(nc, weights, const, vectors, x, p_in, rows, rpb, positions, out, const_at, vector_at, n_blocks):
    with ExitStack() as ctx:
        K = Plan(nc, ctx, const_at, vector_at, n_blocks)
        R = Regions()
        h = K.sbuf("residual", KT * T2).rearrange("p (k n) -> p k n", k=KT)
        R.u, R.y, R.m = K.sbuf("normed", KT * T2), K.sbuf("branch", KT * T2), K.sbuf("mix", KT * T2)
        u, y, R.mix = (a.rearrange("p (k n) -> p k n", k=KT) for a in (R.u, R.y, R.m))
        R.arena = K.sbuf("arena", 10820 + 4096)
        K.n_square = 2
        K.square = K.sbuf("squares", 2 * T2).rearrange("p (i n) -> p i n", i=2)
        K.root = K.sbuf("roots", 2 * T2).rearrange("p (i n) -> p i n", i=2)
        K.sums = K.root[:, 1]
        K.inverse = K.sbuf("inverses", 2 * T2).rearrange("p (i n) -> p i n", i=2)
        K.small = K.sbuf("attention_small", 4)
        mod = K.sbuf("modulation", 2 * 48 * 2).rearrange("p (l m c) -> p l m c", l=2, m=48)
        gains = K.sbuf("gains", 2 * 4 * 16).rearrange("p (l s k c) -> p l s k c", l=2, s=4, k=KT)
        silu = K.sbuf("silu_cond", KT * P).rearrange("p (k n) -> p k n", k=KT)
        R.rows = K.sbuf("decay_rows", 32)
        R.positions = K.sbuf("position_row", S, I32)
        gate = K.sbuf("gates", 64 * 11 + 16 + 128 + 64)
        ga = Area(gate)
        R.gate = {n: ga.get(4, 16) for n in ("x", "mag", "ex", "lg", "g", "beta")}
        R.gate["ea"] = ga.get(16)
        R.gate |= {n: ga.get(2, 4, 8) for n in ("gc", "egc", "ekd", "diff")}
        R.gate |= {"gl_raw": ga.get(2, 4, 16), "gl": ga.get(2, 8, 4)}
        loaded = K.counter("inputs_loaded")
        silued = K.counter("condition")

        vectors_loaded = K.counter("vectors_loaded")

        def load(act):
            act.dma_start(K.vec, vectors).then_inc(vectors_loaded.sem, 16)
            for dst, src in ((K.const, const), (h.rearrange("p k n -> p (k n)"), x), (R.rows, rows.to_broadcast([P, 32])), (R.positions, positions.to_broadcast([P, S]))):
                act.dma_start(dst, src).then_inc(loaded.sem, 16)
        have_vectors = [(vectors_loaded, 16)]
        have = [(loaded, 16 * 4)] + have_vectors
        sb = silued.reserve(1)

        def condition(act):
            need(act, have_vectors)
            cond = K.v("cond").rearrange("p (k c) -> p k c", k=KT)
            for c in range(2):
                ins = act.activation(silu[:, :, 64 * c:64 * c + 64], bc(cond[:, :, c], 2, 64), ACT.Silu)
            ins.then_inc(silued.sem, 1)
        K.add(scalar=load)
        K.add(scalar=condition)
        K.inputs_ready = have
        K.silu_ready = [(silued, sb + 1)]

        def gain_products(layer, slots):
            def todo(dve, step):
                for s in slots:
                    name, part = (("g_pre_mix", 1), ("g_post_mix", 2), ("g_pre_ffn", 4), ("g_post_ffn", 5))[s]
                    m = mod[:, layer, 8 * part:8 * part + 8, :]
                    g = bc(K.v(name)[:, 8 * layer:8 * layer + 8], 2, 2)
                    if s % 2 == 0:
                        step(dve.tensor_scalar(gains[:, layer, s], m, 1.0, None, ALU.add))
                        ins = dve.tensor_tensor(out=gains[:, layer, s], in0=gains[:, layer, s], in1=g, op=ALU.mult)
                    else:
                        ins = dve.tensor_tensor(out=gains[:, layer, s], in0=m, in1=g, op=ALU.mult)
                return ins
            return todo

        def gain(layer, s):
            return lambda k, hf: gains[:, layer, s, k, hf:hf + 1]

        def shift(layer, part):
            return lambda k, hf: mod[:, layer, 8 * part + k, hf:hf + 1]

        r = modulation_stage(K, [Modulation(K, 0, n, silu, mod, 4 + n % 2, 6 + n % 2) for n in range(4)])
        r = gain_stage(K, r + have, gain_products(0, (0,)))
        kr, r = modulated_norm(K, h, T2, 0, gain(0, 0), shift(0, 0), u, r)
        pieces = [lambda a, b, i=i, n=n: Modulation(K, i, n, silu, mod, a, b) for i, n in [(0, n) for n in range(4, 12)] + [(1, n) for n in range(12)]]
        r = even_mixer(K, R, u, r[:0], kr, pieces)
        rest = gain_stage(K, r, gain_products(0, (1, 2, 3)))
        rest = gain_stage(K, rest, gain_products(1, (0, 1, 2, 3)))
        r = r + rest
        r = matmul_stage(K, KT, KT, lambda k: R.mix[:, k, :], T2, lambda e, m, ps: e.activation(y[:, m, :], ps, ACT.Copy), r, squares=True)
        r, tiles = residual(K, h, T2, 0, y, gain(0, 1), r)
        table_ready = []
        for layer in range(2):
            T, lo = (T2, 0) if layer == 0 else (S, S)
            if layer == 1:
                kr, _ = modulated_norm(K, h, T2, 0, gain(1, 0), shift(1, 0), u, [], tiles)
                full = R.arena
                R.arena = full[:, 0:10820]
                R.mixed = full[:, 10820:10820 + KT * S].rearrange("p (k n) -> p k n", k=KT)
                r = odd_mixer(K, R, u, r, kr, table_ready)
                R.arena = full
                r = matmul_stage(K, KT, KT, lambda k: R.mixed[:, k, :], S, lambda e, m, ps: e.activation(y[:, m, 0:S], ps, ACT.Copy), r, squares=True)
                r, tiles = residual(K, h, S, S, y, gain(1, 1), r)
            kr, _ = modulated_norm(K, h, T, lo, gain(layer, 2), shift(layer, 3), u, [], tiles)
            fa = Area(R.arena)
            hidden, tmp = fa.get(22, T), fa.get(2, T)
            if layer == 0:
                R.table = R.m.rearrange("p (h t n) -> p h t n", h=HEADS, t=2)
                table_loaded = bias_load(K, R, rpb, r)
            else:
                R.angle, R.turns, R.quarter, R.dsa_sin, R.dsa_cos = (R.m[:, 2048 + S * i:2048 + S * i + S] for i in range(5))
                R.positions_ready = position_tables(K, R, r)
            r = feed_forward(K, u, T, FF // P, hidden, tmp, y, [], kr, (lambda: table_ready.extend(bias_window(K, R, table_loaded))) if layer == 0 else None)
            r, tiles = residual(K, h, T, lo, y, gain(layer, 3), r)

        lat = h[:, :, S:T2]
        pT = R.u[:, KT * S:KT * S + 4 * S].rearrange("p (l k n) -> p l k n", l=2, k=2)
        p_ready = K.counter("ple_loaded")
        pb = p_ready.reserve(16)
        r0 = r

        def load_p(act):
            need(act, r0)
            act.dma_start(pT, p_in).then_inc(p_ready.sem, 16)
        K.add(scalar=load_p)
        u2 = R.u[:, 0:KT * S].rearrange("p (k n) -> p k n", k=KT)
        y2 = R.y[:, 0:KT * S].rearrange("p (k n) -> p k n", k=KT)
        R.mix2 = R.m[:, 0:KT * S].rearrange("p (k n) -> p k n", k=KT)
        for layer in range(2):
            def plain(name, layer=layer):
                return lambda k, hf: K.v(name)[:, 8 * layer + k:8 * layer + k + 1]
            kr, _ = modulated_norm(K, h, S, S, plain("norm_mix_pre"), None, u2, [], tiles)
            r = sparse_mixer(K, R, layer, u2, r, kr)
            r = matmul_stage(K, KT, KT, lambda k: R.mix2[:, k, :], S, lambda e, m, ps: e.activation(y2[:, m, :], ps, ACT.Copy), r, squares=True)
            r, tiles = residual(K, h, S, S, y2, plain("norm_mix_post"), r)
            kr, _ = modulated_norm(K, h, S, S, plain("norm_mlp_pre"), None, u2, [], tiles)
            hidden = R.arena[:, 0:FF2 // P * S].rearrange("p (k n) -> p k n", n=S)
            sqd = K.counter("hidden_squared")
            made = K.counter("taken_out_by_scalar")
            base = made.n
            r = matmul_stage(K, FF2 // P, KT, lambda k: u2[:, k, :], S, lambda e, m, ps: e.activation(hidden[:, m, :], ps, ACT.Relu), [], k_ready=kr)
            qb = sqd.reserve(FF2 // P)

            def squares(dve, base=base, hidden=hidden):
                for m in range(FF2 // P):
                    dve.wait_ge(made.sem, base + m + 1)
                    dve.tensor_tensor(out=hidden[:, m, :], in0=hidden[:, m, :], in1=hidden[:, m, :], op=ALU.mult).then_inc(sqd.sem, 1)
            K.add(vector=squares)
            r = matmul_stage(K, KT, FF2 // P, lambda k, hidden=hidden: hidden[:, k, :], S, lambda e, m, ps: e.activation(y2[:, m, :], ps, ACT.Copy), r,
                             k_ready=lambda k, qb=qb: [(sqd, qb + k + 1)], squares=True)
            r, tiles = residual(K, h, S, S, y2, plain("norm_mlp_post"), r)
            r = matmul_stage(K, KT, KT, lambda k: lat[:, k, :], S, lambda e, m, ps: e.activation(y2[:, m, :], ps, ACT.Sigmoid), [], k_ready=tiles)

            def embed(dve, m, ps):
                K.in_turn(dve, "vector")(dve.tensor_tensor(out=y2[:, m, :], in0=y2[:, m, :], in1=ps, op=ALU.mult))
                return dve.tensor_tensor(out=lat[:, m, :], in0=lat[:, m, :], in1=y2[:, m, :], op=ALU.add)
            embedded = K.counter("taken_out_by_vector")
            tiles = lambda k, base=embedded.n: [(embedded, base + k + 1)]
            r = matmul_stage(K, KT, 2, lambda k, layer=layer: pT[:, layer, k, :], S, embed, r + [(p_ready, pb + 16)], who=lambda m: "vector")
        stored = K.counter("stored")
        final = r

        def store(sp):
            need(sp, final)
            sp.dma_start(out, lat).then_inc(stored.sem, 16)
            sp.wait_ge(stored.sem, 16)

        assert K.taken == n_blocks, (K.taken, n_blocks)

        block = ctx.enter_context(nc.Block())

        @block.sync
        def _(sp):
            for c in range(K.n_chunks):
                if c >= RING:
                    need(sp, [K.last_use[c - RING]])
                sp.dma_start(K.ring[:, c % RING, :], weights[c]).then_inc(K.chunk_arrived[c % RING].sem, 16)
            store(sp)

        @block.gpsimd
        def _(pool):
            for s in K.programs:
                if "gpsimd" in s:
                    s["gpsimd"](pool)

        @block.scalar
        def _(act):
            for s in K.programs:
                if "scalar" in s:
                    s["scalar"](act)

        @block.vector
        def _(dve):
            for s in K.programs:
                if "vector" in s:
                    s["vector"](dve)

        @block.tensor
        def _(pe):
            for s in K.programs:
                if "tensor" in s:
                    s["tensor"](pe)


def kernel(**inputs):
    import concourse.bacc as bacc
    from concourse.bass_utils import run_bass_kernel_spmd

    x = {k: np.asarray(v) for k, v in inputs.items()}
    blocks = np.concatenate(weight_blocks(x))
    n_blocks = len(blocks)
    pad = -n_blocks % CB
    blocks = np.concatenate([blocks, np.zeros((pad, P, P), np.float32)])
    weights = np.ascontiguousarray(blocks.reshape(-1, CB, P, P).transpose(0, 2, 1, 3)).reshape(-1, P, CB * P)
    parts = constant_parts()
    const_at, n_const = layout({k: v.shape[1] for k, v in parts.items()})
    const = np.concatenate(list(parts.values()), 1)
    vector_at, n_vec = layout(VECTOR_SIZES)
    vp = vector_parts(x)
    vectors = np.concatenate([vp[k] for k in VECTOR_SIZES], 1)
    tokens = np.concatenate([x["ctx"][0], x["x"][0]])
    xT = np.ascontiguousarray(tokens.T.reshape(KT, P, T2).transpose(1, 0, 2)).reshape(P, KT * T2)
    pT = np.ascontiguousarray(x["p_2"][:, 0].reshape(2, S, 2, P).transpose(3, 0, 2, 1))
    rows = np.concatenate([x["gdn_a_log"][0][:, EVEN_ODD].reshape(1, 16), x["gdn_dt_bias"][0][:, EVEN_ODD].reshape(1, 16)], 1)
    arrays = {"weights": weights, "const": const, "vectors": vectors, "tokens": xT, "ple": pT, "rows": np.ascontiguousarray(rows),
              "rpb": np.ascontiguousarray(x["na_rpb"][0]), "positions": np.ascontiguousarray(x["positions_2"])}
    nc = bacc.Bacc("TRN2", target_bir_lowering=False, num_devices=1)
    args = [nc.dram_tensor("in_" + k, a.shape, mybir.dt.from_np(a.dtype), kind="ExternalInput").ap() for k, a in arrays.items()]
    out = nc.dram_tensor("out", (P, KT, S), F32, kind="ExternalOutput").ap()
    program(nc, *args, out, const_at, vector_at, n_blocks)
    r = run_bass_kernel_spmd(nc, [{"in_" + k: a for k, a in arrays.items()}], core_ids=[0])
    o = np.asarray(r.results[0]["out"])
    return np.ascontiguousarray(o.transpose(2, 1, 0)).reshape(1, S, D)
```
